# Optimizing a Trainium2 kernel written in Bass

```python
import jax, jax.numpy as jnp
from jax import lax
import numpy as np

D_MODEL = 1024
BATCH = 1
SEQ = 256
DEPTH = 2

CHUNK = 64
N_A_LAYERS = DEPTH // 2
N_B_LAYERS = DEPTH - N_A_LAYERS
HEAD_DIM = 64
SB_HEADS = D_MODEL // HEAD_DIM
SB_BLOCK = 128
SW_Q_HEADS = D_MODEL // HEAD_DIM
SW_KV_HEADS = max(1, SW_Q_HEADS // 8)
SW_WINDOW = 128
SW_WINDOW_CHUNKS = SW_WINDOW // CHUNK
ROPE_THETA = 10000.0
N_GROUPS = 4
EXPERTS_PER_GROUP = 8
TOP_K_IN_GROUP = 2
EXPERT_FF = D_MODEL // 2
RMS_EPS = 1e-6
NEG_INF = -1e30

kernel_name = "yoco_stickbreak_swa_sink_hmoe"

def rms_norm(x, g):
    xf = x.astype(jnp.float32)
    y = xf * lax.rsqrt(jnp.mean(xf * xf, axis=-1, keepdims=True) + RMS_EPS)
    return (y * g.astype(jnp.float32)).astype(x.dtype)

def rope(x, pos):
    half = HEAD_DIM // 2
    inv = ROPE_THETA ** (-jnp.arange(half, dtype=jnp.float32) / half)
    ang = pos.astype(jnp.float32)[:, None] * inv[None, :]
    cos = jnp.cos(ang)[None, :, None, :]
    sin = jnp.sin(ang)[None, :, None, :]
    xf = x.astype(jnp.float32)
    x1, x2 = xf[..., :half], xf[..., half:]
    out = jnp.concatenate([x1 * cos - x2 * sin, x2 * cos + x1 * sin], axis=-1)
    return out.astype(x.dtype)

def stick_breaking_attention(q, k, v):
    B, S, H, Dh = q.shape
    nb = S // SB_BLOCK
    scale = Dh ** -0.5
    qb = q.reshape(B, nb, SB_BLOCK, H, Dh).transpose(1, 0, 3, 2, 4)
    kpos = jnp.arange(S)

    def block(args):
        qi, bi = args
        z = jnp.einsum('bhqd,bkhd->bhqk', qi, k, preferred_element_type=jnp.float32) * scale
        qpos = bi * SB_BLOCK + jnp.arange(SB_BLOCK)
        causal = kpos[None, :] < qpos[:, None]
        log_beta = jax.nn.log_sigmoid(z)
        log_1m_beta = jnp.where(causal, jax.nn.log_sigmoid(-z), 0.0)
        shifted = jnp.pad(log_1m_beta[..., 1:], ((0, 0), (0, 0), (0, 0), (0, 1)))
        tail = lax.cumsum(shifted, axis=3, reverse=True)
        w = jnp.where(causal, jnp.exp(log_beta + tail), 0.0)
        return jnp.einsum('bhqk,bkhd->bqhd', w.astype(v.dtype), v)

    out = lax.map(block, (qb, jnp.arange(nb)))
    return out.transpose(1, 0, 2, 3, 4).reshape(B, S, H, Dh)

def sliding_window_sink_attention(q, k, v, sinks):
    B, S, Hq, Dh = q.shape
    Hkv = k.shape[2]
    G = Hq // Hkv
    nc = S // CHUNK
    scale = Dh ** -0.5
    qc = q.reshape(B, nc, CHUNK, Hkv, G, Dh)

    def band(t):
        tc = t.reshape(B, nc, CHUNK, Hkv, Dh)
        pieces = [jnp.pad(tc, ((0, 0), (j, 0), (0, 0), (0, 0), (0, 0)))[:, :nc]
                  for j in reversed(range(SW_WINDOW_CHUNKS))]
        return jnp.concatenate(pieces, axis=2)

    kb, vb = band(k), band(v)
    s = jnp.einsum('bcqhgd,bckhd->bchgqk', qc, kb, preferred_element_type=jnp.float32) * scale
    key_chunk_offset = jnp.repeat(jnp.arange(SW_WINDOW_CHUNKS - 1, -1, -1), CHUNK)
    valid = (jnp.arange(nc)[:, None] - key_chunk_offset[None, :]) >= 0
    s = jnp.where(valid[None, :, None, None, None, :], s, NEG_INF)
    sink = sinks.astype(jnp.float32).reshape(Hkv, G)[None, None, :, :, None, None]
    m = jnp.maximum(jnp.max(s, axis=-1, keepdims=True), sink)
    p = jnp.exp(s - m)
    p = p / (jnp.sum(p, axis=-1, keepdims=True) + jnp.exp(sink - m))
    o = jnp.einsum('bchgqk,bckhd->bcqhgd', p.astype(v.dtype), vb)
    return o.reshape(B, S, Hq, Dh)

def hierarchical_moe(x, w_group, b_group, w_router, b_router, w_gate, w_up, w_down):
    B, S, D = x.shape
    xt = x.reshape(B * S, D)
    group_logits = (xt @ w_group).astype(jnp.float32) + b_group.astype(jnp.float32)
    group_probs = jax.nn.softmax(group_logits, axis=-1)
    g_top_p, g_idx = lax.top_k(group_probs, 1)
    group_onehot = jax.nn.one_hot(g_idx[:, 0], N_GROUPS, dtype=jnp.float32)
    expert_logits = jnp.einsum('td,dge->tge', xt, w_router).astype(jnp.float32) + b_router.astype(jnp.float32)
    sel_logits = jnp.einsum('tge,tg->te', expert_logits, group_onehot)
    e_probs = jax.nn.softmax(sel_logits, axis=-1)
    e_top_p, e_idx = lax.top_k(e_probs, TOP_K_IN_GROUP)
    e_top_p = e_top_p / jnp.sum(e_top_p, axis=-1, keepdims=True)
    weights = g_top_p * e_top_p
    exp_w = jnp.sum(jax.nn.one_hot(e_idx, EXPERTS_PER_GROUP, dtype=jnp.float32) * weights[..., None], axis=1)
    combine = (group_onehot[:, :, None] * exp_w[:, None, :]).astype(x.dtype)
    y = jnp.zeros_like(xt)
    for g in range(N_GROUPS):
        h = jax.nn.silu(jnp.einsum('td,edf->tef', xt, w_gate[g])) * jnp.einsum('td,edf->tef', xt, w_up[g])
        y = y + jnp.einsum('tef,efd->td', h * combine[:, g, :, None], w_down[g])
    return y.reshape(B, S, D)

def setup_inputs(seed: int = 0) -> dict:
    key = jax.random.key(seed)
    ks = jax.random.split(key, 20)
    f32 = jnp.float32
    D, NA, NB, L = D_MODEL, N_A_LAYERS, N_B_LAYERS, DEPTH
    G, Eg, F = N_GROUPS, EXPERTS_PER_GROUP, EXPERT_FF

    def nrm(k, shape, scale):
        return jax.random.normal(k, shape, f32) * scale

    def gain(k, shape):
        return 1.0 + 0.02 * jax.random.normal(k, shape, f32)

    sb_w = SB_HEADS * HEAD_DIM
    q_w = SW_Q_HEADS * HEAD_DIM
    kv_w = 2 * SW_KV_HEADS * HEAD_DIM
    return {
        "x": jax.random.normal(ks[0], (BATCH, SEQ, D), f32),
        "a_norm": gain(ks[1], (NA, D)),
        "a_w_qkv": nrm(ks[2], (NA, D, 3 * sb_w), D ** -0.5),
        "a_w_o": nrm(ks[3], (NA, sb_w, D), sb_w ** -0.5),
        "kv_norm": gain(ks[4], (D,)),
        "kv_w": nrm(ks[5], (D, kv_w), D ** -0.5),
        "b_norm": gain(ks[6], (NB, D)),
        "b_w_q": nrm(ks[7], (NB, D, q_w), D ** -0.5),
        "b_sinks": nrm(ks[8], (NB, SW_Q_HEADS), 0.5),
        "b_w_o": nrm(ks[9], (NB, q_w, D), q_w ** -0.5),
        "ffn_norm": gain(ks[10], (L, D)),
        "moe_w_group": nrm(ks[11], (L, D, G), D ** -0.5),
        "moe_b_group": nrm(ks[12], (L, G), 0.01),
        "moe_w_router": nrm(ks[13], (L, D, G, Eg), D ** -0.5),
        "moe_b_router": nrm(ks[14], (L, G, Eg), 0.01),
        "moe_w_gate": nrm(ks[15], (L, G, Eg, D, F), D ** -0.5),
        "moe_w_up": nrm(ks[16], (L, G, Eg, D, F), D ** -0.5),
        "moe_w_down": nrm(ks[17], (L, G, Eg, F, D), F ** -0.5),
        "final_norm": gain(ks[18], (D,)),
    }

def reference(x, a_norm, a_w_qkv, a_w_o, kv_norm, kv_w, b_norm, b_w_q, b_sinks, b_w_o,
              ffn_norm, moe_w_group, moe_b_group, moe_w_router, moe_b_router,
              moe_w_gate, moe_w_up, moe_w_down, final_norm):
    B, S, D = x.shape
    pos = jnp.arange(S, dtype=jnp.int32)
    h = x
    k_shared = None
    v_shared = None
    for layer in range(DEPTH):
        if layer < N_A_LAYERS:
            i = layer
            qkv = rms_norm(h, a_norm[i]) @ a_w_qkv[i]
            q, k, v = jnp.split(qkv, 3, axis=-1)
            shp = (B, S, SB_HEADS, HEAD_DIM)
            o = stick_breaking_attention(q.reshape(shp), k.reshape(shp), v.reshape(shp))
            h = h + o.reshape(B, S, SB_HEADS * HEAD_DIM) @ a_w_o[i]
        else:
            i = layer - N_A_LAYERS
            if i == 0:
                kv = rms_norm(h, kv_norm) @ kv_w
                k_s, v_s = jnp.split(kv, 2, axis=-1)
                k_shared = rope(k_s.reshape(B, S, SW_KV_HEADS, HEAD_DIM), pos)
                v_shared = v_s.reshape(B, S, SW_KV_HEADS, HEAD_DIM)
            q = rope((rms_norm(h, b_norm[i]) @ b_w_q[i]).reshape(B, S, SW_Q_HEADS, HEAD_DIM), pos)
            o = sliding_window_sink_attention(q, k_shared, v_shared, b_sinks[i])
            h = h + o.reshape(B, S, SW_Q_HEADS * HEAD_DIM) @ b_w_o[i]
        h = h + hierarchical_moe(rms_norm(h, ffn_norm[layer]), moe_w_group[layer], moe_b_group[layer],
                                 moe_w_router[layer], moe_b_router[layer], moe_w_gate[layer],
                                 moe_w_up[layer], moe_w_down[layer])
    return rms_norm(h, final_norm)


_drawn_inputs = setup_inputs


def setup_inputs(seed=0):
    import zlib

    import numpy as np

    out = dict(_drawn_inputs(seed))
    spreads = {}
    factors = {'kv_norm': 3.284,
     'b_norm': 7.267,
     'b_sinks': 8.0,
     'moe_b_router': 3.561,
     'final_norm': 2.909}
    for name, (base, spread) in spreads.items():
        noise = np.random.default_rng([zlib.crc32(name.encode()), seed]).standard_normal(out[name].shape)
        drawn = base * np.exp(spread * noise) if base else spread * noise
        out[name] = __import__('jax').numpy.asarray(drawn.astype(out[name].dtype))
    for name, factor in factors.items():
        out[name] = (out[name] * factor).astype(out[name].dtype)
    return out
```

```python
from contextlib import ExitStack

import numpy as np
import concourse.bass as bass
from concourse import mybir

F32 = mybir.dt.float32
I32 = mybir.dt.int32
U32 = mybir.dt.uint32
ALU = mybir.AluOpType
ACT = mybir.ActivationFunctionType
AX = mybir.AxisListType

P = 128
SEQ, D = 256, 1024
T = SEQ // P
KD = D // P
DH = 64
HEADS = D // DH
PAIRS = HEADS // 2
KVH = 2
CHUNK = 64
NCH = SEQ // CHUNK
NG, NE = 4, 8
EXP = NG * NE
FF = D // 2
CAP = 32
QUAD = P // CAP
RING = 8
SLOT = 4096
SLOTS_GROUP = 3 * NE
EPS = 1e-6
FAR = 10000.0
SCALE = DH ** -0.5

C_ID, C_NTRI, C_NONE, C_STRICT, C_CAP, C_ONES = (P * i for i in range(6))
C_MASK = C_STRICT
C_COS = 6 * P
C_SIN = C_COS + T * DH
C_IOTA = C_SIN + T * DH
C_THR = C_IOTA + CAP
N_THR = SEQ // CAP - 1
C_POW = C_THR + 8
N_CONST = C_POW + 8


def bc(ap, axis, n):
    shape = list(ap.shape)
    assert shape[axis] == 1
    shape[axis] = n
    return ap.broadcast_to(shape)


def shape_constants():
    c = np.zeros((P, N_CONST), np.float32)
    row, col = np.arange(P)[:, None], np.arange(P)[None, :]
    c[:, C_ID:C_ID + P] = row == col
    c[:, C_NTRI:C_NTRI + P] = -1.0 * (row >= col)
    c[:, C_NONE:C_NONE + P] = -1.0
    c[:, C_STRICT:C_STRICT + P] = row < col
    c[:, C_ONES:C_ONES + P] = 1.0
    c[:, C_CAP:C_CAP + P] = np.where(row < col, 0.0, -FAR)
    half = DH // 2
    inv = np.float32(10000.0) ** (-np.arange(half, dtype=np.float32) / np.float32(half))
    for t in range(T):
        ang = (np.arange(P) + P * t).astype(np.float32)[:, None] * inv[None, :].astype(np.float32)
        cos, sin = np.cos(ang), np.sin(ang)
        c[:, C_COS + DH * t:C_COS + DH * (t + 1)] = np.concatenate([cos, cos], 1)
        c[:, C_SIN + DH * t:C_SIN + DH * (t + 1)] = np.concatenate([-sin, sin], 1)
    c[:, C_IOTA:C_IOTA + CAP] = np.arange(CAP)
    c[:, C_THR:C_THR + N_THR] = CAP * (1 + np.arange(N_THR))
    c[:, C_POW:C_POW + T] = -0.5
    return c


def build(nc, x, a_norm, a_w_qkv, a_w_o, kv_norm, kv_w, b_norm, b_w_q, b_sinks, b_w_o, ffn_norm,
          moe_w_group, moe_b_group, moe_w_router, moe_b_router, moe_w_gate, moe_w_up, moe_w_down,
          final_norm, consts, out):
    ctx = ExitStack()
    with ctx:
        def sb(name, shape, dt=F32):
            return ctx.enter_context(nc.sbuf_tensor(name, shape, dt))

        def sem(name):
            return ctx.enter_context(nc.semaphore(name))

        ring = sb("ring", [P, RING, SLOT])
        h = sb("h", [P, T, D])
        xn = sb("xn", [P, T, D])
        xT = sb("xT", [P, KD, SEQ])
        oT = sb("oT", [P, KD, SEQ])
        scr = sb("scr", [P, 8704])
        cst = sb("cst", [P, N_CONST])
        gain = sb("gain", [P, 5, KD])
        wr = sb("wr", [P, 2, KD, NG + EXP])
        rbias = sb("rbias", [P, 2, NG + EXP])
        sink16 = sb("sink16", [P, HEADS])
        sinks = sb("sinks", [P, PAIRS])
        ss = sb("ss", [P, 3, T])
        small = sb("small", [P, 512])
        idx8 = sb("idx8", [P, 2, T, 8], U32)
        npass = sb("npass", [P, 2], I32)
        tokw = sb("tokw", [P, T, EXP])
        rank = sb("rank", [P, T, EXP])

        ps = ctx.enter_context(nc.psum_tensor("ps", [P, 8, 512], F32))

        ident = cst[:, C_ID:C_ID + P]
        ntri = cst[:, C_NTRI:C_NTRI + P]
        nones = cst[:, C_NONE:C_NONE + P]
        strict = cst[:, C_STRICT:C_STRICT + P]
        maskc = cst[:, C_MASK:C_MASK + P]
        capc = cst[:, C_CAP:C_CAP + P]
        ones = cst[:, C_ONES:C_ONES + P]
        iota = cst[:, C_IOTA:C_IOTA + CAP]
        v_rows = q_rows = xn
        xTkv = oT
        xg = xT

        at = [0]

        def cut(n):
            at[0] += n
            assert at[0] <= 8704
            return scr[:, at[0] - n:at[0]]

        qT = cut(2 * SEQ).rearrange("p (b q) -> p b q", b=2)
        kz = cut(4 * SEQ).rearrange("p (b a k) -> p b a k", b=2, a=2)
        za = cut(2048).rearrange("p (b a n) -> p b a n", b=2, a=2)
        sp = cut(2048).rearrange("p (b a n) -> p b a n", b=2, a=2)
        wA = cut(2048).rearrange("p (b a n) -> p b a n", b=2, a=2)
        at[0] = 0
        qbd = cut(PAIRS * NCH * P).rearrange("p (m c a q) -> p m c a q", m=PAIRS, c=NCH, a=2)
        k2 = cut(T * KVH * 2 * DH).rearrange("p (t h a d) -> p t h a d", t=T, h=KVH, a=2)
        kdup = cut(KVH * SEQ).rearrange("p (h k) -> p h k", h=KVH)
        vwin = cut(3 * P).rearrange("p (w n) -> p w n", w=3)
        pB = cut(2 * PAIRS * P).rearrange("p (b m k) -> p b m k", b=2, m=PAIRS)
        pT = cut(PAIRS * P).rearrange("p (m n) -> p m n", m=PAIRS)
        ropes = pB.rearrange("p b m k -> p (b m k)").rearrange("p (b r n) -> p b r n", b=2, r=2)
        at[0] = 0
        selg = cut(T * NE * CAP).rearrange("p (t n) -> p t n", t=T)
        selw = cut(T * NE * CAP).rearrange("p (t n) -> p t n", t=T)
        selT = cut(2 * T * P).rearrange("p (q t n) -> p q t n", q=2, t=T)
        sil = cut(2 * P).rearrange("p (b n) -> p b n", b=2)
        hact = cut(2 * P).rearrange("p (b n) -> p b n", b=2)
        hT = cut(2 * P).rearrange("p (b n) -> p b n", b=2)
        yq = cut(2 * D).rearrange("p (q n) -> p q n", q=2)
        at[0] = 0
        fgain = cut(D)

        so = [0]

        def tiny(n):
            so[0] += n
            assert so[0] <= 512
            return small[:, so[0] - n:so[0]]

        logit = tiny(T * (NG + EXP)).rearrange("p (t n) -> p t n", t=T)
        gpad = tiny(T * 8).rearrange("p (t n) -> p t n", t=T)
        gtop8 = tiny(T * 8).rearrange("p (t n) -> p t n", t=T)
        etop8 = tiny(T * 8).rearrange("p (t n) -> p t n", t=T)
        esel = tiny(T * 8).rearrange("p (t n) -> p t n", t=T)
        gidx = tiny(T).rearrange("p (t n) -> p t n", t=T)
        eidx = tiny(2 * T).rearrange("p (t n) -> p t n", t=T)
        goh = tiny(T * NG).rearrange("p (t n) -> p t n", t=T)
        gexp = tiny(T * NG).rearrange("p (t n) -> p t n", t=T)
        gsum = tiny(T)
        oh = tiny(2 * T * NE).rearrange("p (r t n) -> p r t n", r=2, t=T)
        prod = tiny(T * EXP).rearrange("p (t g e) -> p t g e", t=T, g=NG)
        e2 = tiny(T)
        w12 = tiny(2 * T).rearrange("p (r t) -> p r t", r=2)
        wsum = tiny(T * NE).rearrange("p (t n) -> p t n", t=T)
        msum = tiny(T * NE).rearrange("p (t n) -> p t n", t=T)
        member = tiny(T * EXP).rearrange("p (t n) -> p t n", t=T)
        cnt = tiny(2)
        thr = tiny(8)
        mxB = tiny(2 * PAIRS).rearrange("p (b m) -> p b m", b=2)
        esB = tiny(2 * PAIRS).rearrange("p (b m) -> p b m", b=2)

        landed = [sem(f"landed{i}") for i in range(RING)]
        freed = sem("freed")
        x_in = sem("x_in")
        params_in = sem("params_in")
        fgain_in = sem("fgain_in")
        zeroed = sem("zeroed")
        squared = sem("squared")
        var_done = sem("var_done")
        rstd_done = sem("rstd_done")
        xn_done = sem("xn_done")
        xt_psum = sem("xt_psum")
        xt_act = sem("xt_act")
        xt_dve = sem("xt_dve")
        vchain = sem("vchain")
        v_psum = sem("v_psum")
        v_done = sem("v_done")
        qk_psum = sem("qk_psum")
        qk_done = sem("qk_done")
        z_psum = sem("z_psum")
        zabs_done = sem("zabs_done")
        zexp_done = sem("zexp_done")
        zln_done = sem("zln_done")
        sp_done = sem("sp_done")
        tail_psum = sem("tail_psum")
        arg_done = sem("arg_done")
        w_done = sem("w_done")
        o_psum = sem("o_psum")
        o_done = sem("o_done")
        wo_psum = sem("wo_psum")
        h_done = sem("h_done")
        kv_psum = sem("kv_psum")
        kv_done = sem("kv_done")
        kt_psum = sem("kt_psum")
        kt_done = sem("kt_done")
        q_psum = sem("q_psum")
        rope_dve = sem("rope_dve")
        rope_done = sem("rope_done")
        qt_psum = sem("qt_psum")
        qt_act = sem("qt_act")
        qt_dve = sem("qt_dve")
        s_psum = sem("s_psum")
        shifted = sem("shifted")
        p_exp = sem("p_exp")
        p_done = sem("p_done")
        pt_psum = sem("pt_psum")
        pt_done = sem("pt_done")
        ob_psum = sem("ob_psum")
        ob_done = sem("ob_done")
        lg_psum = sem("lg_psum")
        gsub_done = sem("gsub_done")
        gexp_done = sem("gexp_done")
        member_done = sem("member_done")
        rank_psum = sem("rank_psum")
        routed = sem("routed")
        selg_done = sem("selg_done")
        selw_done = sem("selw_done")
        selt_psum = sem("selt_psum")
        selt_done = sem("selt_done")
        xg_psum = sem("xg_psum")
        xg_done = sem("xg_done")
        gu_half = sem("gu_half")
        gu_psum = sem("gu_psum")
        silu_done = sem("silu_done")
        hact_done = sem("hact_done")
        ht_psum = sem("ht_psum")
        ht_done = sem("ht_done")
        y_psum = sem("y_psum")
        y_act = sem("y_act")
        y_dve = sem("y_dve")
        comb_psum = sem("comb_psum")
        added = sem("added")
        moe_done = sem("moe_done")
        stored = sem("stored")

        block = ctx.enter_context(nc.Block())

        SEQ_A, SEQ_M = 0, (8, 13)
        SEQ_B = 8
        N_B = 5

        def slot(s):
            return ring[:, s % RING, :]

        def wait_slot(eng, s, its=0):
            eng.wait_ge(landed[s % RING], its * (32 * SLOTS_GROUP // RING) + 32 * (s // RING + 1))

        @block.sync
        def _(sp_):
            def load(s, parts, its=None):
                if its is not None:
                    sp_.wait_ge(freed, its * SLOTS_GROUP + (s - RING + 1))
                for dst, src in parts:
                    sp_.dma_start(dst, src).then_inc(landed[s % RING], 16)

            def by_k(s, w, c0, n):
                v = w.rearrange("(p k) n -> p k n", p=P)
                t = slot(s)[:, 0:KD * n].rearrange("p (k n) -> p k n", k=KD)
                return [(t[:, 4 * i:4 * i + 4, :], v[:, 4 * i:4 * i + 4, c0:c0 + n]) for i in range(2)]

            def by_m(s, w, c0, n):
                v = w.rearrange("(m p) n -> p m n", p=P)
                t = slot(s).rearrange("p (m n) -> p m n", m=KD)
                return [(t[:, 4 * i:4 * i + 4, :], v[:, 4 * i:4 * i + 4, c0:c0 + n]) for i in range(2)]

            sp_.dma_start(h[:, 0, :], x[0, 0:P, :]).then_inc(x_in, 16)
            sp_.dma_start(h[:, 1, :], x[0, P:SEQ, :]).then_inc(x_in, 16)
            wq = a_w_qkv[0]
            for i in range(2):
                load(i, by_k(i, wq, 2 * D + 512 * i, 512))
            for i in range(4):
                v = wq.rearrange("(p k) n -> p k n", p=P)
                t = slot(2 + i).rearrange("p (k n) -> p k n", k=KD)
                load(2 + i, [(t[:, :, 256 * j:256 * (j + 1)],
                              v[:, :, D * j + 256 * i:D * j + 256 * (i + 1)]) for j in range(2)])
            for i in range(2):
                load(6 + i, by_m(6 + i, a_w_o[0], 512 * i, 512))

            def load_group(layer, g, its):
                for e in range(NE):
                    s = SEQ_M[layer] + 3 * e
                    def of(w, **kw):
                        return w[layer][bass.ds(g, 1), e].rearrange("a (p k) f -> (a p) k f", p=P)
                    for half in range(2):
                        t = slot(s + half).rearrange("p (u k f) -> p u k f", u=2, k=4)
                        load(s + half, [(t[:, u], of(w)[:, 4 * half:4 * half + 4, :])
                                        for u, w in enumerate((moe_w_gate, moe_w_up))], its)
                    t = slot(s + 2).rearrange("p (j n) -> p j n", j=4)
                    wd = moe_w_down[layer][bass.ds(g, 1), e].rearrange("a (j p) n -> (a p) j n", p=P)
                    load(s + 2, [(t[:, 2 * i:2 * i + 2, :], wd[:, 2 * i:2 * i + 2, :])
                                 for i in range(2)], its)

            def load_layer(layer, before):
                with sp_.Fori(0, NG) as g:
                    load_group(layer, g, sp_.snap(g + before))
                sp_.wait_ge(routed, layer + 1)
                n = sp_.value_load(npass[0:1, layer:layer + 1], min_val=1, max_val=SEQ // CAP)
                with sp_.If(n > 1):
                    with sp_.Fori(1, n) as r:
                        with sp_.Fori(0, NG) as g:
                            load_group(layer, g, sp_.snap(r * NG + g + before))
                with sp_.Else():
                    sp_.nop()
                return n

            n1 = load_layer(0, 0)
            its = sp_.snap(n1 * NG)
            load(SEQ_B, by_k(SEQ_B, kv_w, 0, 256), its)
            for i in range(2):
                load(SEQ_B + 1 + i, by_k(SEQ_B + 1 + i, b_w_q[0], 512 * i, 512), its)
            for i in range(2):
                load(SEQ_B + 3 + i, by_m(SEQ_B + 3 + i, b_w_o[0], 512 * i, 512), its)
            load_layer(1, its)
            sp_.wait_ge(xn_done, 5)
            sp_.dma_start(fgain, bc(final_norm.rearrange("(a n) -> a n", a=1), 0, P)
                          ).then_inc(fgain_in, 16)
            for t in range(T):
                sp_.wait_ge(moe_done, 3 + t)
                sp_.dma_start(out[0, P * t:P * (t + 1), :], xn[:, t, :]).then_inc(stored, 16)
            sp_.wait_ge(stored, 16 * T)

        @block.gpsimd
        def _(pool):
            N_PAR = [0]

            def par(dst, src):
                pool.dma_start(dst, src).then_inc(params_in, 16)
                N_PAR[0] += 1

            par(cst[:, :], consts)
            for i, g in enumerate((a_norm[0], ffn_norm[0], kv_norm, b_norm[0], ffn_norm[1])):
                par(gain[:, i, :], g.rearrange("(p k) -> p k", p=P))
            for l in range(2):
                par(wr[:, l, :, 0:NG], moe_w_group[l].rearrange("(p k) g -> p k g", p=P))
                par(wr[:, l, :, NG:], moe_w_router[l].rearrange("(p k) g e -> p k (g e)", p=P))
                par(rbias[:, l, 0:NG], bc(moe_b_group[l:l + 1, :], 0, P))
                par(rbias[:, l, NG:], bc(moe_b_router[l:l + 1].rearrange("a g e -> a (g e)"), 0, P))
            par(sink16[:, :], bc(b_sinks[0:1, :], 0, P))
            assert N_PAR[0] == N_PARAMS
            nc.gpsimd.memset(kz[:, :, :, :], 0.0).then_inc(zeroed, 1)

            def norm(n):
                pool.wait_ge(squared, n + 1)
                if n == 0:
                    pool.wait_ge(params_in, 16 * N_PARAMS)
                nc.gpsimd.tensor_scalar(ss[:, 1, :], ss[:, 0, :], 1.0 / D, EPS, ALU.mult, ALU.add
                                        ).then_inc(var_done, 1)
                pool.wait_ge(var_done, n + 1)
                nc.gpsimd.tensor_tensor(ss[:, 2, :], ss[:, 1, :], cst[:, C_POW:C_POW + T], ALU.pow
                                        ).then_inc(rstd_done, 1)

            def free(done, count):
                pool.wait_ge(done, count)
                pool.sem_inc(freed, 1)

            def free_experts(layer, before):
                pool.wait_ge(routed, layer + 1)
                n = pool.value_load(npass[0:1, layer:layer + 1], min_val=1, max_val=SEQ // CAP)
                with pool.Fori(0, n) as r:
                    with pool.Fori(0, NG) as g:
                        it = pool.snap(r * NG + g + before)
                        for e in range(NE):
                            for done in (gu_half, gu_psum, y_psum):
                                free(done, it * NE + (e + 1))
                return n

            norm(0)
            for i in range(2):
                free(v_psum, 2 * (i + 1))
            for i in range(4):
                free(qk_psum, 2 * (i + 1))
            for i in range(2):
                free(wo_psum, 2 * (i + 1))
            norm(1)
            n1 = free_experts(0, 0)
            norm(2)
            pool.wait_ge(xn_done, 3)
            nc.gpsimd.memset(qbd.rearrange("p m c a q -> p (m c a q)"), 0.0).then_inc(zeroed, 1)
            free(kv_psum, 1)
            pool.wait_ge(xt_psum, 3)
            for i in range(4):
                t, half = i % 2, i // 2
                pool.wait_ge(rope_dve, i + 1)
                nc.gpsimd.tensor_tensor(q_rows[:, t, 512 * half:512 * (half + 1)], ropes[:, i % 2, 0, :],
                                        ropes[:, i % 2, 1, :], ALU.add).then_inc(rope_done, 1)
                if t == T - 1:
                    free(q_psum, i + 1)
            for i in range(2):
                free(wo_psum, 4 + 2 * (i + 1))
            norm(3)
            free_experts(1, pool.snap(n1 * NG))
            norm(4)

        @block.scalar
        def _(act):
            def norm_squares(n):
                if n == 0:
                    act.wait_ge(x_in, 32)
                elif n in (1, 3):
                    act.wait_ge(h_done, 4 * (n // 2 + 1))
                else:
                    act.wait_ge(moe_done, n // 2)
                for t in range(T):
                    last = nc.scalar.activation(xn[:, t, :], h[:, t, :], ACT.Square,
                                                accum_out=ss[:, 0, t:t + 1])
                last.then_inc(squared, 1)

            def norm_store(n, gi, dst):
                act.wait_ge(xt_psum, n + 1)
                if n == 0:
                    act.wait_ge(params_in, 16 * N_PARAMS)
                for k in range(4):
                    last = nc.scalar.activation(dst[:, k, :], ps[:, k // 2, 256 * (k % 2):256 * (k % 2 + 1)],
                                                ACT.Copy, scale=gain[:, gi, k:k + 1])
                return last

            nc.scalar.memzero(idx8[:, 0, 0, 0:1]).then_inc(y_act, 1)

            norm_squares(0)
            norm_store(0, 0, xT).then_inc(xt_act, 1)
            act.wait_ge(zeroed, 1)

            def qk_store(m):
                act.wait_ge(qk_psum, m + 1)
                b = m % 2
                if m >= 2:
                    act.wait_ge(z_psum, m - 1)
                nc.scalar.activation(qT[:, b, :], ps[:, b, 0:SEQ], ACT.Copy, scale=SCALE)
                for a in range(2):
                    r = slice(DH * a, DH * (a + 1))
                    last = nc.scalar.activation(kz[r, b, a, :], ps[r, b, SEQ:2 * SEQ], ACT.Copy)
                last.then_inc(qk_done, 1)

            for i in range(PAIRS + 2):
                if i < PAIRS:
                    qk_store(i)
                if 0 <= i - 1 < PAIRS:
                    m = i - 1
                    act.wait_ge(z_psum, m + 1)
                    if m >= 2:
                        act.wait_ge(sp_done, m - 1)
                    nc.scalar.activation(za[:, m % 2, :, 0:384],
                                         ps[:, 2 + 2 * (m % 2):4 + 2 * (m % 2), 0:384], ACT.Abs
                                         ).then_inc(zabs_done, 1)
                    act.wait_ge(zabs_done, m + 1)
                    nc.scalar.activation(za[:, m % 2, :, 0:384], za[:, m % 2, :, 0:384], ACT.Exp,
                                         scale=-1.0).then_inc(zexp_done, 1)
                    act.wait_ge(zexp_done, m + 1)
                    nc.scalar.activation(za[:, m % 2, :, 0:384], za[:, m % 2, :, 0:384], ACT.Ln,
                                         bias=1.0).then_inc(zln_done, 1)
                if 0 <= i - 2 < PAIRS:
                    m = i - 2
                    act.wait_ge(arg_done, m + 1)
                    nc.scalar.activation(wA[:, m % 2, :, 0:384], wA[:, m % 2, :, 0:384], ACT.Exp
                                         ).then_inc(w_done, 1)

            def moe(layer, before):
                gi = 1 + 3 * layer
                norm_squares(1 + 2 * layer)
                norm_store(1 + 2 * layer, gi, xT).then_inc(xt_act, 1)
                act.wait_ge(gsub_done, 2 * layer + 1)
                nc.scalar.activation(gexp[:, :, :], gexp[:, :, :], ACT.Exp).then_inc(gexp_done, 1)
                act.wait_ge(gsub_done, 2 * layer + 2)
                nc.scalar.activation(e2, e2, ACT.Exp).then_inc(gexp_done, 1)
                act.wait_ge(routed, layer + 1)
                n = act.value_load(npass[0:1, layer:layer + 1], min_val=1, max_val=SEQ // CAP)
                with act.Fori(0, n) as r:
                    with act.Fori(0, NG) as g:
                        it = act.snap(r * NG + g + before)
                        for k in range(KD):
                            act.wait_ge(xg_psum, it * KD + (k + 1))
                            nc.scalar.activation(xg[:, k, :], ps[:, 6 + k % 2, 0:NE * CAP], ACT.Copy,
                                                 scale=gain[:, gi, k:k + 1]).then_inc(xg_done, 1)
                        act.wait_ge(selt_psum, it + 1)
                        nc.scalar.activation(selT.rearrange("p q t n -> p (q t n)"), ps[:, 5, :], ACT.Copy
                                             ).then_inc(selt_done, 1)
                        for e in range(NE):
                            b = e % 2
                            act.wait_ge(gu_psum, it * NE + (e + 1))
                            nc.scalar.activation(sil[:, b, :], ps[:, b, 0:P], ACT.Silu).then_inc(silu_done, 1)
                            act.wait_ge(ht_psum, it * NE + (e + 1))
                            nc.scalar.activation(hT[:, b, :], ps[:, 4, 0:P], ACT.Copy).then_inc(ht_done, 1)
                            act.wait_ge(y_psum, it * NE + (e + 1))
                            r0 = CAP * (e % QUAD)
                            for c in (2, 3):
                                last = nc.scalar.activation(
                                    yq[r0:r0 + CAP, e // QUAD, 256 * c:256 * (c + 1)],
                                    ps[CAP * c:CAP * (c + 1), 2 + b, 0:256], ACT.Copy)
                            last.then_inc(y_act, 1)
                return n

            n1 = moe(0, 0)
            its = act.snap(n1 * NG)

            norm_squares(2)
            norm_store(2, 2, xTkv)
            norm_store(2, 3, xT).then_inc(xt_act, 1)
            act.wait_ge(zeroed, 2)
            for i in range(4):
                act.wait_ge(qt_psum, i + 1)
                t, m0 = i // 2, 4 * (i % 2)
                nc.scalar.activation(qbd[0:DH, m0:m0 + 4, 2 * t:2 * t + 2, 0, :],
                                     ps[0:DH, i, :].rearrange("p (m c q) -> p m c q", m=4, c=2),
                                     ACT.Copy, scale=SCALE).then_inc(qt_act, 1)
            for c in range(NCH):
                b = c % 2
                act.wait_ge(shifted, c + 1)
                w = CHUNK if c == 0 else 2 * CHUNK
                nc.scalar.activation(pB[:, b, :, 0:w], pB[:, b, :, 0:w], ACT.Exp)
                nc.scalar.activation(esB[:, b, :], esB[:, b, :], ACT.Exp).then_inc(p_exp, 1)
                act.wait_ge(pt_psum, c + 1)
                for i in range(2):
                    last = nc.scalar.activation(pT[:, 4 * i:4 * i + 4, :].rearrange("p m n -> p (m n)"),
                                                ps[:, 4 + i, :], ACT.Copy)
                last.then_inc(pt_done, 1)
            moe(1, its)
            norm_squares(4)

        @block.vector
        def _(dve):
            chain = [0]

            def link(ins):
                chain[0] += 1
                ins.then_inc(vchain, 1)
                dve.wait_ge(vchain, chain[0])

            V = nc.vector

            def norm(n, stores):
                dve.wait_ge(rstd_done, n + 1)
                for t in range(T):
                    last = V.tensor_scalar(xn[:, t, :], h[:, t, :], ss[:, 2, t:t + 1], None, ALU.mult)
                last.then_inc(xn_done, 1)
                for gi, dst in stores:
                    dve.wait_ge(xt_psum, n + 1)
                    for k in range(4, 8):
                        last = V.tensor_scalar(dst[:, k, :], ps[:, k // 2, 256 * (k % 2):256 * (k % 2 + 1)],
                                               gain[:, gi, k:k + 1], None, ALU.mult)
                if stores:
                    last.then_inc(xt_dve, 1)

            V.memset(gpad[:, :, :], -3.0e38).then_inc(y_dve, 1)

            dve.wait_ge(x_in, 32)
            dve.wait_ge(params_in, 16 * N_PARAMS)
            norm(0, [(0, xT)])
            for i in range(4):
                t, half = i % 2, i // 2
                dve.wait_ge(v_psum, i + 1)
                V.tensor_copy(v_rows[:, t, 512 * half:512 * (half + 1)], ps[:, 4 + i, :]).then_inc(v_done, 1)

            def diag(x4):
                return x4.rearrange("p a (k n) -> p a k n", k=2)[:, :, :, 0:P]

            def both(c):
                return bc(c.unsqueeze(1), 1, 2)

            for i in range(PAIRS + 3):
                if 0 <= i - 1 < PAIRS:
                    m = i - 1
                    b = m % 2
                    zb = ps[:, 2 + 2 * b:4 + 2 * b, :]
                    dve.wait_ge(zln_done, m + 1)
                    link(V.scalar_tensor_tensor(out=sp[:, b, :, 0:384], in0=zb[:, :, 0:384], scalar=0.0,
                                                in1=za[:, b, :, 0:384], op0=ALU.max, op1=ALU.add))
                    for a in range(2):
                        dg = sp[:, b, a, :].rearrange("p (k n) -> p k n", k=2)[:, :, 0:P]
                        last = V.tensor_tensor(dg, dg, both(maskc), ALU.mult)
                    last.then_inc(sp_done, 1)
                if 0 <= i - 2 < PAIRS:
                    m = i - 2
                    b = m % 2
                    zb = ps[:, 2 + 2 * b:4 + 2 * b, :]
                    dve.wait_ge(tail_psum, m + 1)
                    if m >= 2:
                        dve.wait_ge(o_psum, m - 1)
                    for a in range(2):
                        dg = zb[:, a, :].rearrange("p (k n) -> p k n", k=2)[:, :, 0:P]
                        wd = wA[:, b, a, :].rearrange("p (k n) -> p k n", k=2)[:, :, 0:P]
                        V.tensor_tensor(wd, dg, both(capc), ALU.min)
                    V.tensor_scalar(wA[:, b, :, P:2 * P], zb[:, :, P:2 * P], 0.0, None, ALU.min
                                    ).then_inc(arg_done, 1)
                if 0 <= i - 3 < PAIRS:
                    m = i - 3
                    dve.wait_ge(o_psum, m + 1)
                    V.tensor_copy(oT[:, m, :], ps[:, 6 + m % 2, 0:SEQ]).then_inc(o_done, 1)

            def add_attention(layer):
                for i in range(4):
                    t, half = i % 2, i // 2
                    dve.wait_ge(wo_psum, 4 * layer + i + 1)
                    r = slice(512 * half, 512 * (half + 1))
                    V.tensor_tensor(h[:, t, r], h[:, t, r], ps[:, i, :], ALU.add).then_inc(h_done, 1)

            add_attention(0)

            def spread(x3, n):
                return bc(x3, 2, n)

            def route(layer):
                dve.wait_ge(lg_psum, layer + 1)
                lg = ps[:, 4, 0:T * 64].rearrange("p (t n) -> p t n", t=T)[:, :, 0:NG + EXP]
                link(V.tensor_tensor(logit[:, :, :], lg, bc(rbias[:, layer:layer + 1, :], 1, T), ALU.add))
                link(V.tensor_copy(gpad[:, :, 0:NG], logit[:, :, 0:NG]))
                for t in range(T):
                    last = V.max(gtop8[:, t, :], gpad[:, t, :])
                link(last)
                V.tensor_tensor(gexp[:, :, :], gpad[:, :, 0:NG], spread(gtop8[:, :, 0:1], NG), ALU.subtract
                                ).then_inc(gsub_done, 1)
                for t in range(T):
                    last = V.max_index(idx8[:, 0, t, :], gtop8[:, t, :], gpad[:, t, :])
                link(last)
                link(V.tensor_copy(gidx[:, :, :], idx8[:, 0, :, 0:1]))
                link(V.tensor_tensor(goh[:, :, :], bc(iota[:, 0:NG].unsqueeze(1), 1, T),
                                     spread(gidx[:, :, 0:1], NG), ALU.is_equal))
                link(V.tensor_tensor(prod[:, :, :, :],
                                     logit[:, :, NG:].rearrange("p t (g e) -> p t g e", g=NG),
                                     bc(goh[:, :, :].unsqueeze(3), 3, NE), ALU.mult))
                link(V.tensor_reduce(esel[:, :, :], prod.rearrange("p t g e -> p t e g"), AX.X, ALU.add))
                for t in range(T):
                    last = V.max(etop8[:, t, :], esel[:, t, :])
                link(last)
                V.tensor_tensor(e2.unsqueeze(2), etop8[:, :, 1:2], etop8[:, :, 0:1], ALU.subtract
                                ).then_inc(gsub_done, 1)
                for t in range(T):
                    last = V.max_index(idx8[:, 1, t, :], etop8[:, t, :], esel[:, t, :])
                link(last)
                link(V.tensor_copy(eidx[:, :, :], idx8[:, 1, :, 0:2]))
                for r in range(2):
                    last = V.tensor_tensor(oh[:, r, :, :], bc(iota[:, 0:NE].unsqueeze(1), 1, T),
                                           spread(eidx[:, :, r:r + 1], NE), ALU.is_equal)
                link(last)
                link(V.tensor_tensor(msum[:, :, :], oh[:, 0, :, :], oh[:, 1, :, :], ALU.add))

                def per_group(dst, x3):
                    return V.tensor_tensor(dst.rearrange("p t (g e) -> p t g e", g=NG),
                                           bc(goh[:, :, :].unsqueeze(3), 3, NE),
                                           bc(x3.unsqueeze(2), 2, NG), ALU.mult)

                per_group(member[:, :, :], msum[:, :, :]).then_inc(member_done, 1)
                dve.wait_ge(gexp_done, 2 * layer + 2)
                link(V.tensor_reduce(gsum, gexp[:, :, :], AX.X, ALU.add))
                link(V.tensor_scalar(w12[:, 0, :], e2, 1.0, None, ALU.add))
                link(V.tensor_tensor(w12[:, 0, :], w12[:, 0, :], gsum, ALU.mult))
                link(V.reciprocal(w12[:, 0, :], w12[:, 0, :]))
                link(V.tensor_tensor(w12[:, 1, :], w12[:, 0, :], e2, ALU.mult))
                for r in range(2):
                    last = V.tensor_tensor(oh[:, r, :, :], oh[:, r, :, :],
                                           spread(w12[:, r, :].unsqueeze(2), NE), ALU.mult)
                link(last)
                link(V.tensor_tensor(wsum[:, :, :], oh[:, 0, :, :], oh[:, 1, :, :], ALU.add))
                per_group(tokw[:, :, :], wsum[:, :, :])
                link(V.tensor_scalar(rank[:, :, :], member[:, :, :], -FAR, FAR, ALU.mult, ALU.add))
                dve.wait_ge(rank_psum, layer + 1)
                link(V.tensor_tensor(rank[:, :, :], rank[:, :, :],
                                     ps[:, 5, 0:T * EXP].rearrange("p (t n) -> p t n", t=T), ALU.add))
                link(V.reduce_max(cnt[:, 0:1], ps[:, 5, T * EXP:(T + 1) * EXP], AX.X))
                link(V.tensor_scalar(thr[:, 0:N_THR], cst[:, C_THR:C_THR + N_THR], cnt[:, 0:1], None, ALU.is_lt))
                link(V.tensor_reduce(cnt[:, 1:2], thr[:, 0:N_THR], AX.X, ALU.add))
                V.tensor_scalar(npass[:, layer:layer + 1], cnt[:, 1:2], 1.0, None, ALU.add).then_inc(routed, 1)

            def moe(layer, before):
                norm(1 + 2 * layer, [(1 + 3 * layer, xT)])
                route(layer)
                dve.wait_ge(routed, layer + 1)
                n = dve.value_load(npass[0:1, layer:layer + 1], min_val=1, max_val=SEQ // CAP)

                def add_quad(it, q):
                    for i in range(4):
                        t, half = i // 2, i % 2
                        r = slice(512 * half, 512 * (half + 1))
                        dve.wait_ge(comb_psum, it * 8 + (4 * q + i + 1))
                        V.tensor_tensor(h[:, t, r], h[:, t, r], ps[:, 6 + i % 2, :], ALU.add
                                        ).then_inc(added, 1)

                with dve.Fori(0, n) as r_:
                    with dve.Fori(0, NG) as g:
                        it = dve.snap(r_ * NG + g + before)
                        cols = bass.ds(g * NE, NE)
                        it3 = bc(iota.unsqueeze(1), 1, NE)
                        for t in range(T):
                            last = V.tensor_tensor(selg[:, t, :].rearrange("p (e s) -> p e s", e=NE),
                                                   it3, bc(rank[:, t, cols].unsqueeze(2), 2, CAP),
                                                   ALU.is_equal)
                        last.then_inc(selg_done, 1)
                        dve.wait_ge(selg_done, it + 1)
                        for t in range(T):
                            last = V.tensor_tensor(selw[:, t, :].rearrange("p (e s) -> p e s", e=NE),
                                                   selg[:, t, :].rearrange("p (e s) -> p e s", e=NE),
                                                   bc(tokw[:, t, cols].unsqueeze(2), 2, CAP),
                                                   ALU.mult)
                        last.then_inc(selw_done, 1)
                        V.tensor_scalar(rank[:, :, cols], rank[:, :, cols], float(-CAP), None, ALU.add)
                        for e in range(NE):
                            b = e % 2
                            dve.wait_ge(silu_done, it * NE + (e + 1))
                            V.tensor_tensor(hact[:, b, :], sil[:, b, :], ps[:, b, P:2 * P], ALU.mult
                                            ).then_inc(hact_done, 1)
                            if e == QUAD:
                                add_quad(it, 0)
                            dve.wait_ge(y_psum, it * NE + (e + 1))
                            r0 = CAP * (e % QUAD)
                            for c in (0, 1):
                                last = V.tensor_copy(yq[r0:r0 + CAP, e // QUAD, 256 * c:256 * (c + 1)],
                                                     ps[CAP * c:CAP * (c + 1), 2 + b, 0:256])
                            last.then_inc(y_dve, 1)
                        add_quad(it, 1)
                link(V.tensor_copy(cnt[:, 0:1], cnt[:, 1:2]))
                V.tensor_copy(cnt[:, 1:2], cnt[:, 0:1]).then_inc(moe_done, 1)
                return n

            n1 = moe(0, 0)
            its = dve.snap(n1 * NG)

            norm(2, [(2, xTkv), (3, xT)])

            def rope(dst, src, tmp, t, nh):
                def c3(c0, a, b):
                    return bc(cst[:, c0 + DH * t + a:c0 + DH * t + b].unsqueeze(1), 1, nh)
                hd = DH // 2
                V.tensor_tensor(dst, src, c3(C_COS, 0, DH), ALU.mult)
                V.tensor_tensor(tmp[:, :, 0:hd], src[:, :, hd:DH], c3(C_SIN, 0, hd), ALU.mult)
                return V.tensor_tensor(tmp[:, :, hd:DH], src[:, :, 0:hd], c3(C_SIN, hd, DH), ALU.mult)

            kvt = ps[:, 4, :].rearrange("p (t n) -> p t n", t=T)
            dve.wait_ge(kv_psum, 1)
            for t in range(T):
                ka, kb = (ropes[:, 0, r, 128 * t:128 * (t + 1)].rearrange("p (h d) -> p h d", h=KVH)
                          for r in range(2))
                link(rope(ka, kvt[:, t, 0:P].rearrange("p (h d) -> p h d", h=KVH), kb, t, KVH))
                for a in range(2):
                    last = V.tensor_tensor(k2[:, t, :, a, :], ka, kb, ALU.add)
            V.tensor_copy(vwin[:, 0, :], kvt[:, 0, P:2 * P])
            V.tensor_copy(vwin[:, 2, :], kvt[:, 1, P:2 * P])
            V.tensor_copy(vwin[0:DH, 1, :], kvt[DH:P, 0, P:2 * P])
            V.tensor_copy(vwin[DH:P, 1, :], kvt[0:DH, 1, P:2 * P]).then_inc(kv_done, 1)
            dve.wait_ge(kt_psum, 1)
            V.tensor_copy(kdup.rearrange("p h k -> p (h k)"), ps[:, 5, :]).then_inc(kt_done, 1)
            for i in range(4):
                t, half = i % 2, i // 2
                dve.wait_ge(q_psum, i + 1)
                if i >= 2:
                    dve.wait_ge(rope_done, i - 1)
                rope(ropes[:, i % 2, 0, :].rearrange("p (h d) -> p h d", h=8),
                     ps[:, i, :].rearrange("p (h d) -> p h d", h=8),
                     ropes[:, i % 2, 1, :].rearrange("p (h d) -> p h d", h=8), t, 8).then_inc(rope_dve, 1)
            dve.wait_ge(zeroed, 2)
            for i in range(4):
                dve.wait_ge(qt_psum, i + 1)
                t, m0 = i // 2, 4 * (i % 2)
                V.tensor_scalar(qbd[DH:P, m0:m0 + 4, 2 * t:2 * t + 2, 1, :],
                                ps[DH:P, i, :].rearrange("p (m c q) -> p m c q", m=4, c=2),
                                SCALE, None, ALU.mult).then_inc(qt_dve, 1)
            for a in range(2):
                V.tensor_copy(sinks[DH * a:DH * (a + 1), :],
                              sink16[DH * a:DH * (a + 1), :].rearrange("p (m a) -> p m a", a=2)[:, :, a])
            link(V.memset(pB[:, 0, :, CHUNK:2 * CHUNK], 0.0))
            for c in range(NCH):
                b = c % 2
                w = CHUNK if c == 0 else 2 * CHUNK
                sc = ps[:, 2 * b:2 * b + 2, :].rearrange("p x (m k) -> p (x m) k", m=4)[:, :, 0:w]
                dve.wait_ge(s_psum, c + 1)
                link(V.tensor_reduce(mxB[:, b, :], sc, AX.X, ALU.max))
                link(V.tensor_tensor(mxB[:, b, :], mxB[:, b, :], sinks[:, :], ALU.max))
                if c >= 2:
                    dve.wait_ge(pt_psum, c - 1)
                V.tensor_tensor(esB[:, b, :], sinks[:, :], mxB[:, b, :], ALU.subtract)
                V.tensor_tensor(pB[:, b, :, 0:w], sc, bc(mxB[:, b, :].unsqueeze(2), 2, w),
                                ALU.subtract).then_inc(shifted, 1)
                dve.wait_ge(p_exp, c + 1)
                link(V.tensor_reduce(mxB[:, b, :], pB[:, b, :, 0:w], AX.X, ALU.add))
                link(V.tensor_tensor(mxB[:, b, :], mxB[:, b, :], esB[:, b, :], ALU.add))
                link(V.reciprocal(mxB[:, b, :], mxB[:, b, :]))
                V.tensor_tensor(pB[:, b, :, 0:w], pB[:, b, :, 0:w],
                                bc(mxB[:, b, :].unsqueeze(2), 2, w), ALU.mult).then_inc(p_done, 1)
                if c >= 1:
                    dve.wait_ge(ob_psum, c)
                    V.tensor_copy(oT[:, :, CHUNK * (c - 1):CHUNK * c],
                                  ps[:, 6 + (c - 1) % 2, :].rearrange("p (m q) -> p m q", m=PAIRS)
                                  ).then_inc(ob_done, 1)
            dve.wait_ge(ob_psum, NCH)
            V.tensor_copy(oT[:, :, CHUNK * (NCH - 1):], ps[:, 6 + (NCH - 1) % 2, :].rearrange(
                "p (m q) -> p m q", m=PAIRS)).then_inc(ob_done, 1)
            add_attention(1)
            moe(1, its)
            norm(4, [])
            dve.wait_ge(xn_done, 5)
            dve.wait_ge(fgain_in, 16)
            for t in range(T):
                V.tensor_tensor(xn[:, t, :], xn[:, t, :], fgain, ALU.mult).then_inc(moe_done, 1)

        @block.tensor
        def _(pe):
            MM = nc.tensor.matmul

            def transpose_rows(n):
                pe.wait_ge(xn_done, n + 1)
                for k in range(KD):
                    for t in range(T):
                        c0 = 256 * (k % 2) + P * t
                        last = nc.tensor.transpose(ps[:, k // 2, c0:c0 + P], xn[:, t, k::KD], ident)
                last.then_inc(xt_psum, 1)
                pe.wait_ge(xt_act, n + 1)
                pe.wait_ge(xt_dve, n + 1)

            pe.wait_ge(params_in, 16 * N_PARAMS)
            transpose_rows(0)
            for i in range(4):
                t, half = i % 2, i // 2
                s = SEQ_A + half
                wait_slot(pe, s)
                wv = slot(s).rearrange("p (k n) -> p k n", k=KD)
                for k in range(KD):
                    last = MM(ps[:, 4 + i, :], xT[:, k, P * t:P * (t + 1)], wv[:, k, :],
                              start=k == 0, stop=k == KD - 1)
                last.then_inc(v_psum, 1)

            for i in range(PAIRS + 3):
                if i < PAIRS:
                    m = i
                    s = SEQ_A + 2 + m // 2
                    wait_slot(pe, s)
                    if m >= 2:
                        pe.wait_ge(qk_done, m - 1)
                    w = slot(s).rearrange("p (k n) -> p k n", k=KD)
                    for j in range(2):
                        for k in range(KD):
                            c0 = 256 * j + P * (m % 2)
                            last = MM(ps[:, m % 2, SEQ * j:SEQ * (j + 1)], w[:, k, c0:c0 + P], xT[:, k, :],
                                      start=k == 0, stop=k == KD - 1)
                    last.then_inc(qk_psum, 1)
                if 0 <= i - 1 < PAIRS:
                    m = i - 1
                    b = m % 2
                    pe.wait_ge(qk_done, m + 1)
                    if m < 2:
                        pe.wait_ge(v_done, 2 * b + 2 if b == 0 else 4)
                    else:
                        pe.wait_ge(arg_done, m - 1)
                    for a in range(2):
                        z = ps[:, 2 + 2 * b + a, :]
                        MM(z[:, 0:SEQ], kz[:, b, a, 0:P], qT[:, b, :], start=True, stop=False,
                           skip_group_check=True)
                        last = MM(z[:, SEQ:SEQ + P], kz[:, b, a, P:SEQ], qT[:, b, P:SEQ], start=False,
                                  stop=False, skip_group_check=True)
                    last.then_inc(z_psum, 1)
                if 0 <= i - 2 < PAIRS:
                    m = i - 2
                    b = m % 2
                    pe.wait_ge(sp_done, m + 1)
                    for a in range(2):
                        z = ps[:, 2 + 2 * b + a, :]
                        s0 = sp[:, b, a, :]
                        MM(z[:, SEQ:SEQ + P], ntri, s0[:, SEQ:SEQ + P], start=False, stop=False,
                           skip_group_check=True)
                        MM(z[:, 0:SEQ], ntri, s0[:, 0:SEQ], start=False, stop=False, skip_group_check=True)
                        last = MM(z[:, P:SEQ], nones, s0[:, SEQ:SEQ + P], start=False, stop=True,
                                  skip_group_check=True)
                    last.then_inc(tail_psum, 1)
                if 0 <= i - 3 < PAIRS:
                    m = i - 3
                    b = m % 2
                    pe.wait_ge(w_done, m + 1)
                    pe.wait_ge(v_done, 4)
                    if m >= 2:
                        pe.wait_ge(o_done, m - 1)
                    for kt in range(2):
                        for a in range(2):
                            hd = 2 * m + a
                            last = MM(ps[DH * a:DH * (a + 1), 6 + b, P * kt:SEQ],
                                      v_rows[:, kt, DH * hd:DH * (hd + 1)],
                                      wA[:, b, a, SEQ * kt:SEQ if kt == 0 else SEQ + P],
                                      start=kt == 0, stop=kt == 1, skip_group_check=True)
                    last.then_inc(o_psum, 1)

            def project_out(seq, its):
                for i in range(4):
                    t, half = i % 2, i // 2
                    wait_slot(pe, seq + half, its)
                    w = slot(seq + half).rearrange("p (m n) -> p m n", m=KD)
                    for m in range(KD):
                        last = MM(ps[:, i, :], oT[:, m, P * t:P * (t + 1)], w[:, m, :],
                                  start=m == 0, stop=m == KD - 1)
                    last.then_inc(wo_psum, 1)

            pe.wait_ge(o_done, PAIRS)
            project_out(SEQ_A + 6, 0)

            def moe(layer, before):
                seq = SEQ_M[layer]
                pe.wait_ge(h_done, 4 * (layer + 1))
                transpose_rows(1 + 2 * layer)
                for t in range(T):
                    for k in range(KD):
                        last = MM(ps[:, 4, 64 * t:64 * t + NG + EXP], xT[:, k, P * t:P * (t + 1)],
                                  wr[:, layer, k, :], start=k == 0, stop=k == KD - 1)
                last.then_inc(lg_psum, 1)
                pe.wait_ge(member_done, layer + 1)
                MM(ps[:, 5, 0:EXP], strict, member[:, 0, :], start=True, stop=True)
                MM(ps[:, 5, EXP:2 * EXP], strict, member[:, 1, :], start=True, stop=False)
                MM(ps[:, 5, EXP:2 * EXP], ones, member[:, 0, :], start=False, stop=True)
                MM(ps[:, 5, 2 * EXP:3 * EXP], ones, member[:, 0, :], start=True, stop=False)
                MM(ps[:, 5, 2 * EXP:3 * EXP], ones, member[:, 1, :], start=False, stop=True
                   ).then_inc(rank_psum, 1)
                pe.wait_ge(routed, layer + 1)
                n = pe.value_load(npass[0:1, layer:layer + 1], min_val=1, max_val=SEQ // CAP)

                def combine(it, q):
                    pe.wait_ge(y_act, it * NE + (QUAD * (q + 1) + 1))
                    pe.wait_ge(y_dve, it * NE + (QUAD * (q + 1) + 1))
                    if q == 0:
                        pe.wait_ge(selt_done, it + 1)
                    for i in range(4):
                        t, half = i // 2, i % 2
                        if i >= 2:
                            pe.wait_ge(added, it * 8 + (4 * q + i - 1))
                        elif q == 1 and i == 0:
                            pe.wait_ge(added, it * 8 + 4)
                        MM(ps[:, 6 + i % 2, :], selT[:, q, t, :], yq[:, q, 512 * half:512 * (half + 1)],
                           start=True, stop=True).then_inc(comb_psum, 1)

                with pe.Fori(0, n) as r:
                    with pe.Fori(0, NG) as g:
                        it = pe.snap(r * NG + g + before)
                        pe.wait_ge(selg_done, it + 1)
                        for k in range(KD):
                            if k >= 2:
                                pe.wait_ge(xg_done, it * KD + (k - 1))
                            for t in range(T):
                                last = MM(ps[:, 6 + k % 2, 0:NE * CAP], xn[:, t, k::KD], selg[:, t, :],
                                          start=t == 0, stop=t == T - 1)
                            last.then_inc(xg_psum, 1)
                        pe.wait_ge(selw_done, it + 1)
                        for q in range(2):
                            for t in range(T):
                                last = nc.tensor.transpose(ps[:, 5, P * (2 * q + t):P * (2 * q + t + 1)],
                                                           selw[:, t, P * q:P * (q + 1)], ident)
                        last.then_inc(selt_psum, 1)
                        pe.wait_ge(xg_done, it * KD + KD)
                        for e in range(NE):
                            b = e % 2
                            s = seq + 3 * e
                            for half in range(2):
                                wait_slot(pe, s + half, it)
                                w = slot(s + half).rearrange("p (u k f) -> p u k f", u=2, k=4)
                                for k in range(4):
                                    for j in range(4):
                                        kk = 4 * half + k
                                        last = MM(ps[CAP * j:CAP * (j + 1), b, 0:2 * P].rearrange(
                                                      "p (u f) -> p u f", u=2),
                                                  xg[:, kk, CAP * e:CAP * (e + 1)],
                                                  w[:, :, k, P * j:P * (j + 1)],
                                                  start=kk == 0, stop=kk == KD - 1, skip_group_check=True)
                                last.then_inc(gu_psum if half else gu_half, 1)
                            if e == QUAD:
                                combine(it, 0)
                            pe.wait_ge(hact_done, it * NE + (e + 1))
                            nc.tensor.transpose(ps[:, 4, 0:P], hact[:, b, :], ident).then_inc(ht_psum, 1)
                            pe.wait_ge(ht_done, it * NE + (e + 1))
                            pe.wait_ge(y_act, it * NE + (e + 1))
                            pe.wait_ge(y_dve, it * NE + (e + 1))
                            wait_slot(pe, s + 2, it)
                            w = slot(s + 2).rearrange("p (j n) -> p j n", j=4)
                            for j in range(4):
                                for c in range(4):
                                    last = MM(ps[CAP * c:CAP * (c + 1), 2 + b, 0:256],
                                              hT[:, b, CAP * j:CAP * (j + 1)],
                                              w[:, j, 256 * c:256 * (c + 1)],
                                              start=j == 0, stop=j == 3, skip_group_check=True)
                            last.then_inc(y_psum, 1)
                        combine(it, 1)
                return n

            n1 = moe(0, 0)
            its = pe.snap(n1 * NG)

            transpose_rows(2)
            wait_slot(pe, SEQ_B, its)
            w = slot(SEQ_B)[:, 0:KD * 256].rearrange("p (k n) -> p k n", k=KD)
            for t in range(T):
                for k in range(KD):
                    last = MM(ps[:, 4, 256 * t:256 * (t + 1)], xTkv[:, k, P * t:P * (t + 1)], w[:, k, :],
                              start=k == 0, stop=k == KD - 1)
            last.then_inc(kv_psum, 1)
            for i in range(4):
                t, half = i % 2, i // 2
                s = SEQ_B + 1 + half
                wait_slot(pe, s, its)
                w = slot(s).rearrange("p (k n) -> p k n", k=KD)
                for k in range(KD):
                    last = MM(ps[:, i, :], xT[:, k, P * t:P * (t + 1)], w[:, k, :],
                              start=k == 0, stop=k == KD - 1)
                last.then_inc(q_psum, 1)
            pe.wait_ge(kv_done, 1)
            for hk in range(KVH):
                for t in range(T):
                    c0 = SEQ * hk + P * t
                    last = nc.tensor.transpose(ps[:, 5, c0:c0 + P],
                                               k2[:, t, hk, :, :].rearrange("p a d -> p (a d)"), ident)
            last.then_inc(kt_psum, 1)
            pe.wait_ge(rope_done, 4)
            for i in range(4):
                t, m0 = i // 2, 4 * (i % 2)
                for m in range(4):
                    last = nc.tensor.transpose(ps[:, i, P * m:P * (m + 1)],
                                               q_rows[:, t, P * (m0 + m):P * (m0 + m + 1)], ident)
                last.then_inc(qt_psum, 1)
            pe.wait_ge(kt_done, 1)
            pe.wait_ge(qt_act, 4)
            pe.wait_ge(qt_dve, 4)

            def scores(c):
                b = c % 2
                if c >= 2:
                    pe.wait_ge(shifted, c - 1)
                k0 = max(0, CHUNK * (c - 1))
                for m in range(PAIRS):
                    last = MM(ps[:, 2 * b + m // 4, P * (m % 4):P * (m % 4 + 1)],
                              qbd[:, m, c, :, :].rearrange("p a q -> p (a q)"),
                              kdup[:, m // (PAIRS // KVH), k0:k0 + P], start=True, stop=True)
                last.then_inc(s_psum, 1)

            scores(0)
            for c in range(NCH):
                b = c % 2
                if c + 1 < NCH:
                    scores(c + 1)
                pe.wait_ge(p_done, c + 1)
                if c >= 1:
                    pe.wait_ge(pt_done, c)
                for m in range(PAIRS):
                    last = nc.tensor.transpose(ps[:, 4 + m // 4, P * (m % 4):P * (m % 4 + 1)],
                                               pB[:, b, m, :], ident)
                last.then_inc(pt_psum, 1)
                pe.wait_ge(pt_done, c + 1)
                if c >= 2:
                    pe.wait_ge(ob_done, c - 1)
                win = max(0, c - 1)
                for hk in range(KVH):
                    for a in range(2):
                        last = MM(ps[DH * a:DH * (a + 1), 6 + b, 256 * hk:256 * (hk + 1)].rearrange(
                                      "p (m q) -> p m q", m=4),
                                  vwin[:, win, DH * hk:DH * (hk + 1)],
                                  pT[:, 4 * hk:4 * hk + 4, DH * a:DH * (a + 1)],
                                  start=True, stop=True, skip_group_check=True)
                last.then_inc(ob_psum, 1)
            pe.wait_ge(ob_done, NCH)
            project_out(SEQ_B + 3, its)
            moe(1, its)


N_PARAMS = 1 + 5 + 8 + 1

_INS = ["x", "a_norm", "a_w_qkv", "a_w_o", "kv_norm", "kv_w", "b_norm", "b_w_q", "b_sinks", "b_w_o",
        "ffn_norm", "moe_w_group", "moe_b_group", "moe_w_router", "moe_b_router", "moe_w_gate",
        "moe_w_up", "moe_w_down", "final_norm"]


def kernel(**inputs):
    import concourse.bacc as bacc
    from concourse.bass_utils import run_bass_kernel_spmd

    nc = bacc.Bacc("TRN2", target_bir_lowering=False, num_devices=1)
    arrays = {f"in_{n}": np.ascontiguousarray(inputs[n]) for n in _INS}
    arrays["in_consts"] = shape_constants()
    args = [nc.dram_tensor(n, a.shape, mybir.dt.from_np(a.dtype), kind="ExternalInput").ap()
            for n, a in arrays.items()]
    args.append(nc.dram_tensor("out_0", (1, SEQ, D), F32, kind="ExternalOutput").ap())
    build(nc, *args)
    r = run_bass_kernel_spmd(nc, [arrays], core_ids=[0])
    return r.results[0]["out_0"]
```

```python
from contextlib import ExitStack

import numpy as np
import concourse.bass as bass
from concourse import mybir

F32 = mybir.dt.float32
BF16 = mybir.dt.bfloat16
I32 = mybir.dt.int32
U32 = mybir.dt.uint32
ALU = mybir.AluOpType
ACT = mybir.ActivationFunctionType
AX = mybir.AxisListType

P = 128
SEQ, D = 256, 1024
T = SEQ // P
KD = D // P
DH = 64
HEADS = D // DH
PAIRS = HEADS // 2
KVH = 2
CHUNK = 64
NCH = SEQ // CHUNK
NG, NE = 4, 8
EXP = NG * NE
FF = D // 2
CAP = 32
QUAD = P // CAP
RING = 8
SLOT = 4096
SLOTS_GROUP = 3 * NE
EPS = 1e-6
FAR = 10000.0
SCALE = DH ** -0.5

C_ID, C_NTRI, C_NONE, C_STRICT, C_CAP, C_ONES = (P * i for i in range(6))
C_MASK = C_STRICT
C_COS = 6 * P
C_SIN = C_COS + T * DH
C_IOTA = C_SIN + T * DH
C_THR = C_IOTA + CAP
N_THR = SEQ // CAP - 1
C_POW = C_THR + 8
N_CONST = C_POW + 8


def bc(ap, axis, n):
    shape = list(ap.shape)
    assert shape[axis] == 1
    shape[axis] = n
    return ap.broadcast_to(shape)


def shape_constants():
    c = np.zeros((P, N_CONST), np.float32)
    row, col = np.arange(P)[:, None], np.arange(P)[None, :]
    c[:, C_ID:C_ID + P] = row == col
    c[:, C_NTRI:C_NTRI + P] = -1.0 * (row >= col)
    c[:, C_NONE:C_NONE + P] = -1.0
    c[:, C_STRICT:C_STRICT + P] = row < col
    c[:, C_ONES:C_ONES + P] = 1.0
    c[:, C_CAP:C_CAP + P] = np.where(row < col, 0.0, -FAR)
    half = DH // 2
    inv = np.float32(10000.0) ** (-np.arange(half, dtype=np.float32) / np.float32(half))
    for t in range(T):
        ang = (np.arange(P) + P * t).astype(np.float32)[:, None] * inv[None, :].astype(np.float32)
        cos, sin = np.cos(ang), np.sin(ang)
        c[:, C_COS + DH * t:C_COS + DH * (t + 1)] = np.concatenate([cos, cos], 1)
        c[:, C_SIN + DH * t:C_SIN + DH * (t + 1)] = np.concatenate([-sin, sin], 1)
    c[:, C_IOTA:C_IOTA + CAP] = np.arange(CAP)
    c[:, C_THR:C_THR + N_THR] = CAP * (1 + np.arange(N_THR))
    c[:, C_POW:C_POW + T] = -0.5
    return c


def build(nc, x, a_norm, a_w_qkv, a_w_o, kv_norm, kv_w, b_norm, b_w_q, b_sinks, b_w_o, ffn_norm,
          moe_w_group, moe_b_group, moe_w_router, moe_b_router, moe_w_gate, moe_w_up, moe_w_down,
          final_norm, consts, out):
    ctx = ExitStack()
    with ctx:
        def sb(name, shape, dt=F32):
            return ctx.enter_context(nc.sbuf_tensor(name, shape, dt))

        def sem(name):
            return ctx.enter_context(nc.semaphore(name))

        ring = sb("ring", [P, RING, SLOT])
        h = sb("h", [P, T, D])
        xn = sb("xn", [P, T, D])
        xT = sb("xT", [P, KD, SEQ])
        oT = sb("oT", [P, KD, SEQ])
        scr = sb("scr", [P, 8704])
        cst = sb("cst", [P, N_CONST])
        gain = sb("gain", [P, 5, KD])
        wr_in = sb("wr_in", [P, 2, KD * (NG + EXP)])
        wr = sb("wr", [P, 2, KD, NG + EXP])
        rbias = sb("rbias", [P, 2, NG + EXP])
        sink16 = sb("sink16", [P, HEADS])
        sinks = sb("sinks", [P, PAIRS])
        ss = sb("ss", [P, 3, T])
        counting = sb("counting", [P, 2, P], BF16)
        member = sb("member", [P, T, EXP], BF16)
        small = sb("small", [P, 512])
        idx8 = sb("idx8", [P, 2, T, 8], U32)
        npass = sb("npass", [P, 2], I32)
        tokw = sb("tokw", [P, T, EXP])
        rank = sb("rank", [P, T, EXP])

        ps = ctx.enter_context(nc.psum_tensor("ps", [P, 8, 512], F32))

        ident = cst[:, C_ID:C_ID + P]
        ntri = cst[:, C_NTRI:C_NTRI + P]
        nones = cst[:, C_NONE:C_NONE + P]
        strict = cst[:, C_STRICT:C_STRICT + P]
        maskc = cst[:, C_MASK:C_MASK + P]
        capc = cst[:, C_CAP:C_CAP + P]
        ones = cst[:, C_ONES:C_ONES + P]
        iota = cst[:, C_IOTA:C_IOTA + CAP]
        v_rows = q_rows = xn
        xTkv = oT
        xg = xT

        at = [0]

        def cut(n):
            at[0] += n
            assert at[0] <= 8704
            return scr[:, at[0] - n:at[0]]

        qT = cut(2 * SEQ).rearrange("p (b q) -> p b q", b=2)
        kz = cut(4 * SEQ).rearrange("p (b a k) -> p b a k", b=2, a=2)
        za = cut(2048).rearrange("p (b a n) -> p b a n", b=2, a=2)
        sp = cut(2048).rearrange("p (b a n) -> p b a n", b=2, a=2)
        wA = cut(2048).rearrange("p (b a n) -> p b a n", b=2, a=2)
        at[0] = 0
        k2 = cut(T * KVH * 2 * DH).rearrange("p (t h a d) -> p t h a d", t=T, h=KVH, a=2)
        kdup = cut(KVH * SEQ).rearrange("p (h k) -> p h k", h=KVH)
        vwin = cut(3 * P).rearrange("p (w n) -> p w n", w=3)
        pB = cut(2 * PAIRS * P).rearrange("p (b m k) -> p b m k", b=2, m=PAIRS)
        pT = cut(PAIRS * P).rearrange("p (m n) -> p m n", m=PAIRS)
        ropes = pB.rearrange("p b m k -> p (b m k)").rearrange("p (b r n) -> p b r n", b=2, r=2)
        at[0] = 8704 - PAIRS * NCH * P
        assert at[0] >= 4352
        qbd = cut(PAIRS * NCH * P).rearrange("p (m c a q) -> p m c a q", m=PAIRS, c=NCH, a=2)
        at[0] = 0
        selg = cut(T * NE * CAP).rearrange("p (t n) -> p t n", t=T)
        selw = cut(T * NE * CAP).rearrange("p (t n) -> p t n", t=T)
        selT = cut(2 * T * P).rearrange("p (q t n) -> p q t n", q=2, t=T)
        sil = cut(2 * P).rearrange("p (b n) -> p b n", b=2)
        hact = cut(2 * P).rearrange("p (b n) -> p b n", b=2)
        hT = cut(2 * P).rearrange("p (b n) -> p b n", b=2)
        yq = cut(2 * D).rearrange("p (q n) -> p q n", q=2)
        at[0] = 8704 - D
        fgain = cut(D)

        so = [0]

        def tiny(n):
            so[0] += n
            assert so[0] <= 512
            return small[:, so[0] - n:so[0]]

        logit = tiny(T * (NG + EXP)).rearrange("p (t n) -> p t n", t=T)
        gpad = tiny(T * 8).rearrange("p (t n) -> p t n", t=T)
        gtop8 = tiny(T * 8).rearrange("p (t n) -> p t n", t=T)
        etop8 = tiny(T * 8).rearrange("p (t n) -> p t n", t=T)
        esel = tiny(T * 8).rearrange("p (t n) -> p t n", t=T)
        gidx = tiny(T).rearrange("p (t n) -> p t n", t=T)
        eidx = tiny(2 * T).rearrange("p (t n) -> p t n", t=T)
        goh = tiny(T * NG).rearrange("p (t n) -> p t n", t=T)
        gexp = tiny(T * NG).rearrange("p (t n) -> p t n", t=T)
        gsum = tiny(T)
        oh = tiny(2 * T * NE).rearrange("p (r t n) -> p r t n", r=2, t=T)
        prod = tiny(T * EXP).rearrange("p (t g e) -> p t g e", t=T, g=NG)
        e2 = tiny(T)
        w12 = tiny(2 * T).rearrange("p (r t) -> p r t", r=2)
        wsum = tiny(T * NE).rearrange("p (t n) -> p t n", t=T)
        msum = tiny(T * NE).rearrange("p (t n) -> p t n", t=T)
        cnt = tiny(2)
        thr = tiny(8)
        mxB = tiny(2 * PAIRS).rearrange("p (b m) -> p b m", b=2)
        esB = tiny(2 * PAIRS).rearrange("p (b m) -> p b m", b=2)

        landed = [sem(f"landed{i}") for i in range(RING)]
        freed = sem("freed")
        x_in = [sem(f"x_in{t}") for t in range(T)]
        const_in = sem("const_in")
        params_in = sem("params_in")
        prepared = sem("prepared")
        fgain_in = sem("fgain_in")
        zeroed = sem("zeroed")
        squared = sem("squared")
        var_done = sem("var_done")
        rstd_done = sem("rstd_done")
        xn_done = sem("xn_done")
        out_done = sem("out_done")
        xt_psum = sem("xt_psum")
        xt_act = sem("xt_act")
        xt_dve = sem("xt_dve")
        vchain = sem("vchain")
        v_psum = sem("v_psum")
        v_done = sem("v_done")
        qk_psum = sem("qk_psum")
        qk_done = sem("qk_done")
        z_psum = sem("z_psum")
        zabs_done = sem("zabs_done")
        zexp_done = sem("zexp_done")
        zln_done = sem("zln_done")
        sp_done = sem("sp_done")
        tail_psum = sem("tail_psum")
        arg_done = sem("arg_done")
        w_done = sem("w_done")
        o_psum = sem("o_psum")
        o_done = sem("o_done")
        wo_psum = sem("wo_psum")
        h_done = sem("h_done")
        kv_psum = sem("kv_psum")
        kv_done = sem("kv_done")
        kt_psum = sem("kt_psum")
        kt_done = sem("kt_done")
        q_psum = sem("q_psum")
        rope_dve = sem("rope_dve")
        rope_done = sem("rope_done")
        qt_psum = sem("qt_psum")
        qt_act = sem("qt_act")
        qt_dve = sem("qt_dve")
        s_psum = sem("s_psum")
        shifted = sem("shifted")
        p_exp = sem("p_exp")
        p_done = sem("p_done")
        pt_psum = sem("pt_psum")
        pt_done = sem("pt_done")
        ob_psum = sem("ob_psum")
        ob_done = sem("ob_done")
        lg_psum = sem("lg_psum")
        gsub_done = sem("gsub_done")
        gexp_done = sem("gexp_done")
        member_done = sem("member_done")
        rank_psum = sem("rank_psum")
        routed = sem("routed")
        selg_done = sem("selg_done")
        selw_done = sem("selw_done")
        selt_psum = sem("selt_psum")
        selt_done = sem("selt_done")
        xg_psum = sem("xg_psum")
        xg_done = sem("xg_done")
        gu_half = sem("gu_half")
        gu_psum = sem("gu_psum")
        silu_done = sem("silu_done")
        hact_done = sem("hact_done")
        ht_psum = sem("ht_psum")
        ht_done = sem("ht_done")
        y_psum = sem("y_psum")
        y_act = sem("y_act")
        y_dve = sem("y_dve")
        comb_psum = sem("comb_psum")
        added = [sem(f"added{t}") for t in range(T)]
        counted = sem("counted")
        stored = sem("stored")

        block = ctx.enter_context(nc.Block())

        WO_BANKS = ((0, 1, 2, 3), (7, 2, 3, 7))

        SEQ_A, SEQ_M = 0, (8, 13)
        SEQ_B = 8
        N_B = 5

        def slot(s):
            return ring[:, s % RING, :]

        def wait_slot(eng, s, its=0):
            eng.wait_ge(landed[s % RING], its * (32 * SLOTS_GROUP // RING) + 32 * (s // RING + 1))

        def rows_stand(eng, n, t, its=None):
            if n == 0:
                eng.wait_ge(x_in[t], 16)
            elif n % 2:
                eng.wait_ge(h_done, 4 * (n // 2) + 2 * (t + 1))
            else:
                eng.wait_ge(added[t], its * 4)

        def passes(eng, layer, before, group):
            with eng.Fori(0, NG) as g:
                group(g, eng.snap(g + before))
            eng.wait_ge(routed, layer + 1)
            n = eng.value_load(npass[0:1, layer:layer + 1], min_val=1, max_val=SEQ // CAP)
            with eng.If(n > 1):
                with eng.Fori(1, n) as r:
                    with eng.Fori(0, NG) as g:
                        group(g, eng.snap(r * NG + g + before))
            with eng.Else():
                eng.nop()
            return n

        @block.sync
        def _(sp_):
            def load(s, parts, its=None):
                if its is not None:
                    sp_.wait_ge(freed, its * SLOTS_GROUP + (s - RING + 1))
                for dst, src in parts:
                    sp_.dma_start(dst, src).then_inc(landed[s % RING], 16)

            def by_k(s, w, c0, n):
                v = w.rearrange("(p k) n -> p k n", p=P)
                t = slot(s)[:, 0:KD * n].rearrange("p (k n) -> p k n", k=KD)
                return [(t[:, 4 * i:4 * i + 4, :], v[:, 4 * i:4 * i + 4, c0:c0 + n]) for i in range(2)]

            def by_m(s, w, c0, n):
                v = w.rearrange("(m p) n -> p m n", p=P)
                t = slot(s).rearrange("p (m n) -> p m n", m=KD)
                return [(t[:, 4 * i:4 * i + 4, :], v[:, 4 * i:4 * i + 4, c0:c0 + n]) for i in range(2)]

            for t in range(T):
                sp_.dma_start(h[:, t, :], x[0, P * t:P * (t + 1), :]).then_inc(x_in[t], 16)
            sp_.dma_start(cst[:, :], consts).then_inc(const_in, 16)
            sp_.dma_start(gain[:, 0, :], a_norm[0].rearrange("(p k) -> p k", p=P)).then_inc(const_in, 16)
            wq = a_w_qkv[0]
            for i in range(2):
                load(i, by_k(i, wq, 2 * D + 512 * i, 512))
            for i in range(4):
                v = wq.rearrange("(p k) n -> p k n", p=P)
                t = slot(2 + i).rearrange("p (k n) -> p k n", k=KD)
                load(2 + i, [(t[:, :, 256 * j:256 * (j + 1)],
                              v[:, :, D * j + 256 * i:D * j + 256 * (i + 1)]) for j in range(2)])
            for i in range(2):
                load(6 + i, by_m(6 + i, a_w_o[0], 512 * i, 512))

            pars = [(gain[:, 1 + i, :], g.rearrange("(p k) -> p k", p=P))
                    for i, g in enumerate((ffn_norm[0], kv_norm, b_norm[0], ffn_norm[1]))]
            for l in range(2):
                pars += [(wr_in[:, l, 0:KD * NG], moe_w_group[l].rearrange("(p k) g -> p (k g)", p=P)),
                         (wr_in[:, l, KD * NG:], moe_w_router[l].rearrange("(p k) g e -> p (k g e)", p=P)),
                         (rbias[:, l, 0:NG], bc(moe_b_group[l:l + 1, :], 0, P)),
                         (rbias[:, l, NG:], bc(moe_b_router[l:l + 1].rearrange("a g e -> a (g e)"), 0, P))]
            pars.append((sink16[:, :], bc(b_sinks[0:1, :], 0, P)))
            assert len(pars) == N_PARAMS
            for dst, src in pars:
                sp_.dma_start(dst, src).then_inc(params_in, 16)

            def load_group(layer, g, its):
                for e in range(NE):
                    s = SEQ_M[layer] + 3 * e
                    def of(w, **kw):
                        return w[layer][bass.ds(g, 1), e].rearrange("a (p k) f -> (a p) k f", p=P)
                    for half in range(2):
                        t = slot(s + half).rearrange("p (u k f) -> p u k f", u=2, k=4)
                        load(s + half, [(t[:, u], of(w)[:, 4 * half:4 * half + 4, :])
                                        for u, w in enumerate((moe_w_gate, moe_w_up))], its)
                    t = slot(s + 2).rearrange("p (j n) -> p j n", j=4)
                    wd = moe_w_down[layer][bass.ds(g, 1), e].rearrange("a (j p) n -> (a p) j n", p=P)
                    load(s + 2, [(t[:, 2 * i:2 * i + 2, :], wd[:, 2 * i:2 * i + 2, :])
                                 for i in range(2)], its)

            def load_layer(layer, before):
                return passes(sp_, layer, before, lambda g, it: load_group(layer, g, it))

            n1 = load_layer(0, 0)
            its = sp_.snap(n1 * NG)
            load(SEQ_B, by_k(SEQ_B, kv_w, 0, 256), its)
            for i in range(2):
                load(SEQ_B + 1 + i, by_k(SEQ_B + 1 + i, b_w_q[0], 512 * i, 512), its)
            for i in range(2):
                load(SEQ_B + 3 + i, by_m(SEQ_B + 3 + i, b_w_o[0], 512 * i, 512), its)
            load_layer(1, its)
            for t in range(T):
                sp_.wait_ge(out_done, t + 1)
                sp_.dma_start(out[0, P * t:P * (t + 1), :], xn[:, t, :]).then_inc(stored, 16)
            sp_.wait_ge(stored, 16 * T)

        @block.gpsimd
        def _(pool):
            nc.gpsimd.memset(kz[:, :, :, :], 0.0).then_inc(zeroed, 1)

            def norm(n):
                pool.wait_ge(squared, T * (n + 1))
                if n == 0:
                    pool.wait_ge(const_in, 32)
                nc.gpsimd.tensor_scalar(ss[:, 1, :], ss[:, 0, :], 1.0 / D, EPS, ALU.mult, ALU.add
                                        ).then_inc(var_done, 1)
                pool.wait_ge(var_done, n + 1)
                nc.gpsimd.tensor_tensor(ss[:, 2, :], ss[:, 1, :], cst[:, C_POW:C_POW + T], ALU.pow
                                        ).then_inc(rstd_done, 1)

            def free(done, count):
                pool.wait_ge(done, count)
                pool.sem_inc(freed, 1)

            def free_experts(layer, before):
                pool.wait_ge(counted, layer + 1)
                nc.gpsimd.tensor_copy(npass[:, layer:layer + 1], cnt[:, 1:2]).then_inc(routed, 1)

                def free_group(g, it):
                    for e in range(NE):
                        for done in (gu_half, gu_psum, y_psum):
                            free(done, it * NE + (e + 1))

                return passes(pool, layer, before, free_group)

            norm(0)
            for i in range(2):
                free(v_psum, 2 * (i + 1))
            for i in range(4):
                free(qk_psum, 2 * (i + 1))
            pool.wait_ge(params_in, 16 * N_PARAMS)
            for l, gi in enumerate((1, 4)):
                for c0, n0, n in ((0, 0, NG), (KD * NG, NG, EXP)):
                    nc.gpsimd.tensor_tensor(
                        wr[:, l, :, n0:n0 + n],
                        wr_in[:, l, c0:c0 + KD * n].rearrange("p (k n) -> p k n", k=KD),
                        bc(gain[:, gi, :].unsqueeze(2), 2, n), ALU.mult)
            nc.gpsimd.tensor_copy(counting[:, 0, :], strict)
            nc.gpsimd.tensor_copy(counting[:, 1, :], ones).then_inc(prepared, 1)
            for i in range(2):
                free(wo_psum, 3 + i)
            norm(1)
            nc.gpsimd.memset(qbd.rearrange("p m c a q -> p (m c a q)"), 0.0).then_inc(zeroed, 1)
            n1 = free_experts(0, 0)
            norm(2)
            free(kv_psum, 1)
            for i in range(4):
                t, half = i // 2, i % 2
                pool.wait_ge(rope_dve, i + 1)
                nc.gpsimd.tensor_tensor(q_rows[:, t, 512 * half:512 * (half + 1)], ropes[:, i % 2, 0, :],
                                        ropes[:, i % 2, 1, :], ALU.add).then_inc(rope_done, 1)
                if t == T - 1:
                    free(q_psum, i + 1)
            for i in range(2):
                free(wo_psum, 4 + 3 + i)
            norm(3)
            pool.dma_start(fgain, bc(final_norm.rearrange("(a n) -> a n", a=1), 0, P)
                           ).then_inc(fgain_in, 16)
            free_experts(1, pool.snap(n1 * NG))
            norm(4)

        @block.scalar
        def _(act):
            def norm_squares(n, its=None):
                for t in range(T):
                    rows_stand(act, n, t, its)
                    nc.scalar.activation(xn[:, t, :], h[:, t, :], ACT.Square,
                                         accum_out=ss[:, 0, t:t + 1]).then_inc(squared, 1)

            def store_transposed(n, gains):
                for t in range(T):
                    act.wait_ge(xt_psum, T * n + t + 1)
                    for gi, dst in gains:
                        src = ps[:, 2 * t, :].rearrange("p (k q) -> p k q", k=4)
                        if gi is None:
                            last = nc.scalar.activation(dst[:, 0:4, P * t:P * (t + 1)], src, ACT.Copy)
                            continue
                        for k in range(4):
                            last = nc.scalar.activation(dst[:, k, P * t:P * (t + 1)], src[:, k, :], ACT.Copy,
                                                        scale=gain[:, gi, k:k + 1])
                    last.then_inc(xt_act, 1)

            nc.scalar.memzero(idx8[:, 0, 0, 0:1]).then_inc(y_act, 1)

            norm_squares(0)
            act.wait_ge(const_in, 32)
            store_transposed(0, [(0, xT)])
            act.wait_ge(zeroed, 1)

            def qk_store(m):
                act.wait_ge(qk_psum, m + 1)
                b = m % 2
                if m >= 2:
                    act.wait_ge(z_psum, m - 1)
                nc.scalar.activation(qT[:, b, :], ps[:, b, 0:SEQ], ACT.Copy, scale=SCALE)
                for a in range(2):
                    r = slice(DH * a, DH * (a + 1))
                    last = nc.scalar.activation(kz[r, b, a, :], ps[r, b, SEQ:2 * SEQ], ACT.Copy)
                last.then_inc(qk_done, 1)

            for i in range(PAIRS + 2):
                if i < PAIRS:
                    qk_store(i)
                if 0 <= i - 1 < PAIRS:
                    m = i - 1
                    act.wait_ge(z_psum, m + 1)
                    if m >= 2:
                        act.wait_ge(sp_done, m - 1)
                    nc.scalar.activation(za[:, m % 2, :, 0:384],
                                         ps[:, 2 + 2 * (m % 2):4 + 2 * (m % 2), 0:384], ACT.Abs
                                         ).then_inc(zabs_done, 1)
                    act.wait_ge(zabs_done, m + 1)
                    nc.scalar.activation(za[:, m % 2, :, 0:384], za[:, m % 2, :, 0:384], ACT.Exp,
                                         scale=-1.0).then_inc(zexp_done, 1)
                    act.wait_ge(zexp_done, m + 1)
                    nc.scalar.activation(za[:, m % 2, :, 0:384], za[:, m % 2, :, 0:384], ACT.Ln,
                                         bias=1.0).then_inc(zln_done, 1)
                if 0 <= i - 2 < PAIRS:
                    m = i - 2
                    act.wait_ge(arg_done, m + 1)
                    nc.scalar.activation(wA[:, m % 2, :, 0:384], wA[:, m % 2, :, 0:384], ACT.Exp
                                         ).then_inc(w_done, 1)

            def moe(layer, before):
                gi = 1 + 3 * layer
                norm_squares(1 + 2 * layer)
                store_transposed(1 + 2 * layer, [(None, xT)])
                act.wait_ge(rstd_done, 2 + 2 * layer)
                for t in range(T):
                    nc.scalar.activation(xn[:, t, :], h[:, t, :], ACT.Copy, scale=ss[:, 2, t:t + 1]
                                         ).then_inc(xn_done, 1)
                act.wait_ge(gsub_done, 2 * layer + 1)
                nc.scalar.activation(gexp[:, :, :], gexp[:, :, :], ACT.Exp).then_inc(gexp_done, 1)
                act.wait_ge(gsub_done, 2 * layer + 2)
                nc.scalar.activation(e2, e2, ACT.Exp).then_inc(gexp_done, 1)

                def group(g, it):
                    for k in range(KD):
                        act.wait_ge(xg_psum, it * KD + (k + 1))
                        nc.scalar.activation(xg[:, k, :], ps[:, 6 + k % 2, 0:NE * CAP], ACT.Copy,
                                             scale=gain[:, gi, k:k + 1]).then_inc(xg_done, 1)
                    act.wait_ge(selt_psum, it + 1)
                    nc.scalar.activation(selT.rearrange("p q t n -> p (q t n)"), ps[:, 5, :], ACT.Copy
                                         ).then_inc(selt_done, 1)
                    for e in range(NE):
                        b = e % 2
                        act.wait_ge(gu_psum, it * NE + (e + 1))
                        nc.scalar.activation(sil[:, b, :], ps[:, b, 0:P], ACT.Silu).then_inc(silu_done, 1)
                        act.wait_ge(ht_psum, it * NE + (e + 1))
                        nc.scalar.activation(hT[:, b, :], ps[:, 4, 0:P], ACT.Copy).then_inc(ht_done, 1)
                        act.wait_ge(y_psum, it * NE + (e + 1))
                        r0 = CAP * (e % QUAD)
                        for c in (2, 3):
                            last = nc.scalar.activation(
                                yq[r0:r0 + CAP, e // QUAD, 256 * c:256 * (c + 1)],
                                ps[CAP * c:CAP * (c + 1), 2 + b, 0:256], ACT.Copy)
                        last.then_inc(y_act, 1)

                return passes(act, layer, before, group)

            n1 = moe(0, 0)
            its = act.snap(n1 * NG)

            norm_squares(2, its)
            store_transposed(2, [(2, xTkv), (3, xT)])
            act.wait_ge(zeroed, 2)

            def store_q(i):
                act.wait_ge(qt_psum, i + 1)
                t, m0 = i // 2, 4 * (i % 2)
                nc.scalar.activation(qbd[0:DH, m0:m0 + 4, 2 * t:2 * t + 2, 0, :],
                                     ps[0:DH, i, :].rearrange("p (m c q) -> p m c q", m=4, c=2),
                                     ACT.Copy, scale=SCALE).then_inc(qt_act, 1)

            def exp_scores(c):
                b = c % 2
                w = CHUNK if c == 0 else 2 * CHUNK
                act.wait_ge(shifted, c + 1)
                nc.scalar.activation(pB[:, b, :, 0:w], pB[:, b, :, 0:w], ACT.Exp)
                nc.scalar.activation(esB[:, b, :], esB[:, b, :], ACT.Exp).then_inc(p_exp, 1)

            def store_pT(c):
                act.wait_ge(pt_psum, c + 1)
                for i in range(2):
                    last = nc.scalar.activation(pT[:, 4 * i:4 * i + 4, :].rearrange("p m n -> p (m n)"),
                                                ps[:, 4 + i, :], ACT.Copy)
                last.then_inc(pt_done, 1)

            store_q(0)
            store_q(1)
            exp_scores(0)
            exp_scores(1)
            store_pT(0)
            store_q(2)
            store_q(3)
            exp_scores(2)
            store_pT(1)
            exp_scores(3)
            store_pT(2)
            store_pT(3)
            n2 = moe(1, its)
            norm_squares(4, act.snap((n1 + n2) * NG))

        @block.vector
        def _(dve):
            chain = [0]

            def link(ins):
                chain[0] += 1
                ins.then_inc(vchain, 1)
                dve.wait_ge(vchain, chain[0])

            V = nc.vector

            def store_transposed(n, gains):
                for t in range(T):
                    dve.wait_ge(xt_psum, T * n + t + 1)
                    for gi, dst in gains:
                        src = ps[:, 2 * t + 1, :].rearrange("p (k q) -> p k q", k=4)
                        d = dst[:, 4:8, P * t:P * (t + 1)]
                        if gi is None:
                            last = V.tensor_copy(d, src)
                        else:
                            last = V.tensor_tensor(d, src, bc(gain[:, gi, 4:8].unsqueeze(2), 2, P), ALU.mult)
                    last.then_inc(xt_dve, 1)

            V.memset(gpad[:, :, :], -3.0e38).then_inc(y_dve, 1)

            dve.wait_ge(rstd_done, 1)
            for t in range(T):
                V.tensor_scalar(xn[:, t, :], h[:, t, :], ss[:, 2, t:t + 1], None, ALU.mult
                                ).then_inc(xn_done, 1)
            dve.wait_ge(const_in, 32)
            store_transposed(0, [(0, xT)])
            for i in range(4):
                t, half = i % 2, i // 2
                dve.wait_ge(v_psum, i + 1)
                V.tensor_copy(v_rows[:, t, 512 * half:512 * (half + 1)], ps[:, 4 + i, :]).then_inc(v_done, 1)

            def diag(x4):
                return x4.rearrange("p a (k n) -> p a k n", k=2)[:, :, :, 0:P]

            def both(c):
                return bc(c.unsqueeze(1), 1, 2)

            for i in range(PAIRS + 3):
                if 0 <= i - 1 < PAIRS:
                    m = i - 1
                    b = m % 2
                    zb = ps[:, 2 + 2 * b:4 + 2 * b, :]
                    dve.wait_ge(zln_done, m + 1)
                    link(V.scalar_tensor_tensor(out=sp[:, b, :, 0:384], in0=zb[:, :, 0:384], scalar=0.0,
                                                in1=za[:, b, :, 0:384], op0=ALU.max, op1=ALU.add))
                    for a in range(2):
                        dg = sp[:, b, a, :].rearrange("p (k n) -> p k n", k=2)[:, :, 0:P]
                        last = V.tensor_tensor(dg, dg, both(maskc), ALU.mult)
                    last.then_inc(sp_done, 1)
                if 0 <= i - 2 < PAIRS:
                    m = i - 2
                    b = m % 2
                    zb = ps[:, 2 + 2 * b:4 + 2 * b, :]
                    dve.wait_ge(tail_psum, m + 1)
                    if m >= 2:
                        dve.wait_ge(o_psum, m - 1)
                    for a in range(2):
                        dg = zb[:, a, :].rearrange("p (k n) -> p k n", k=2)[:, :, 0:P]
                        wd = wA[:, b, a, :].rearrange("p (k n) -> p k n", k=2)[:, :, 0:P]
                        V.tensor_tensor(wd, dg, both(capc), ALU.min)
                    V.tensor_scalar(wA[:, b, :, P:2 * P], zb[:, :, P:2 * P], 0.0, None, ALU.min
                                    ).then_inc(arg_done, 1)
                if 0 <= i - 3 < PAIRS:
                    m = i - 3
                    dve.wait_ge(o_psum, m + 1)
                    V.tensor_copy(oT[:, m, :], ps[:, 6 + m % 2, 0:SEQ]).then_inc(o_done, 1)

            def add_attention(layer, i):
                r = slice(512 * (i % 2), 512 * (i % 2 + 1))
                dve.wait_ge(wo_psum, 4 * layer + i + 1)
                V.tensor_tensor(h[:, i // 2, r], h[:, i // 2, r], ps[:, WO_BANKS[layer][i], :], ALU.add
                                ).then_inc(h_done, 1)

            for i in range(4):
                add_attention(0, i)

            def spread(x3, n):
                return bc(x3, 2, n)

            def route(layer):
                dve.wait_ge(lg_psum, layer + 1)
                lg = ps[:, 4, 0:T * 64].rearrange("p (t n) -> p t n", t=T)[:, :, 0:NG + EXP]
                dve.wait_ge(rstd_done, 2 + 2 * layer)
                for t in range(T):
                    for dst, c in ((gpad[:, t, 0:NG], slice(0, NG)), (logit[:, t, NG:], slice(NG, NG + EXP))):
                        last = V.scalar_tensor_tensor(out=dst, in0=lg[:, t, c], scalar=ss[:, 2, t:t + 1],
                                                      in1=rbias[:, layer, c], op0=ALU.mult, op1=ALU.add)
                link(last)
                for t in range(T):
                    last = V.max(gtop8[:, t, :], gpad[:, t, :])
                link(last)
                V.tensor_tensor(gexp[:, :, :], gpad[:, :, 0:NG], spread(gtop8[:, :, 0:1], NG), ALU.subtract
                                ).then_inc(gsub_done, 1)
                for t in range(T):
                    last = V.max_index(idx8[:, 0, t, :], gtop8[:, t, :], gpad[:, t, :])
                link(last)
                link(V.tensor_copy(gidx[:, :, :], idx8[:, 0, :, 0:1]))
                link(V.tensor_tensor(goh[:, :, :], bc(iota[:, 0:NG].unsqueeze(1), 1, T),
                                     spread(gidx[:, :, 0:1], NG), ALU.is_equal))
                link(V.tensor_tensor(prod[:, :, :, :],
                                     logit[:, :, NG:].rearrange("p t (g e) -> p t g e", g=NG),
                                     bc(goh[:, :, :].unsqueeze(3), 3, NE), ALU.mult))
                link(V.tensor_reduce(esel[:, :, :], prod.rearrange("p t g e -> p t e g"), AX.X, ALU.add))
                for t in range(T):
                    last = V.max(etop8[:, t, :], esel[:, t, :])
                link(last)
                V.tensor_tensor(e2.unsqueeze(2), etop8[:, :, 1:2], etop8[:, :, 0:1], ALU.subtract
                                ).then_inc(gsub_done, 1)
                for t in range(T):
                    last = V.max_index(idx8[:, 1, t, :], etop8[:, t, :], esel[:, t, :])
                link(last)
                link(V.tensor_copy(eidx[:, :, :], idx8[:, 1, :, 0:2]))
                for r in range(2):
                    last = V.tensor_tensor(oh[:, r, :, :], bc(iota[:, 0:NE].unsqueeze(1), 1, T),
                                           spread(eidx[:, :, r:r + 1], NE), ALU.is_equal)
                link(last)
                link(V.tensor_tensor(msum[:, :, :], oh[:, 0, :, :], oh[:, 1, :, :], ALU.add))

                def per_group(dst, x3):
                    return V.tensor_tensor(dst.rearrange("p t (g e) -> p t g e", g=NG),
                                           bc(goh[:, :, :].unsqueeze(3), 3, NE),
                                           bc(x3.unsqueeze(2), 2, NG), ALU.mult)

                per_group(member[:, :, :], msum[:, :, :]).then_inc(member_done, 1)
                dve.wait_ge(gexp_done, 2 * layer + 2)
                link(V.tensor_reduce(gsum, gexp[:, :, :], AX.X, ALU.add))
                link(V.tensor_scalar(w12[:, 0, :], e2, 1.0, None, ALU.add))
                link(V.tensor_tensor(w12[:, 0, :], w12[:, 0, :], gsum, ALU.mult))
                link(V.reciprocal(w12[:, 0, :], w12[:, 0, :]))
                link(V.tensor_tensor(w12[:, 1, :], w12[:, 0, :], e2, ALU.mult))
                for r in range(2):
                    last = V.tensor_tensor(oh[:, r, :, :], oh[:, r, :, :],
                                           spread(w12[:, r, :].unsqueeze(2), NE), ALU.mult)
                link(last)
                link(V.tensor_tensor(wsum[:, :, :], oh[:, 0, :, :], oh[:, 1, :, :], ALU.add))
                per_group(tokw[:, :, :], wsum[:, :, :])
                link(V.tensor_scalar(rank[:, :, :], member[:, :, :], -FAR, FAR, ALU.mult, ALU.add))
                dve.wait_ge(rank_psum, layer + 1)
                link(V.tensor_tensor(rank[:, :, :], rank[:, :, :],
                                     ps[:, 5, 0:T * EXP].rearrange("p (t n) -> p t n", t=T), ALU.add))
                link(V.reduce_max(cnt[:, 0:1], ps[:, 5, T * EXP:(T + 1) * EXP], AX.X))
                V.tensor_scalar(thr[:, 0:N_THR], cst[:, C_THR:C_THR + N_THR], cnt[:, 0:1], 1.0,
                                ALU.is_lt, ALU.add, accum_out=cnt[:, 1:2]).then_inc(counted, 1)

            def moe(layer, before):
                store_transposed(1 + 2 * layer, [(None, xT)])
                route(layer)

                def add_quad(it, q):
                    for i in range(4):
                        t, half = i // 2, i % 2
                        r = slice(512 * half, 512 * (half + 1))
                        dve.wait_ge(comb_psum, it * 8 + (4 * q + i + 1))
                        V.tensor_tensor(h[:, t, r], h[:, t, r], ps[:, 6 + i % 2, :], ALU.add
                                        ).then_inc(added[t], 1)

                def group(g, it):
                    cols = bass.ds(g * NE, NE)
                    slots = bc(iota.unsqueeze(1), 1, NE)
                    for t in range(T):
                        last = V.tensor_tensor(selg[:, t, :].rearrange("p (e s) -> p e s", e=NE),
                                               slots, bc(rank[:, t, cols].unsqueeze(2), 2, CAP),
                                               ALU.is_equal)
                    last.then_inc(selg_done, 1)
                    dve.wait_ge(selg_done, it + 1)
                    for t in range(T):
                        last = V.tensor_tensor(selw[:, t, :].rearrange("p (e s) -> p e s", e=NE),
                                               selg[:, t, :].rearrange("p (e s) -> p e s", e=NE),
                                               bc(tokw[:, t, cols].unsqueeze(2), 2, CAP),
                                               ALU.mult)
                    last.then_inc(selw_done, 1)
                    V.tensor_scalar(rank[:, :, cols], rank[:, :, cols], float(-CAP), None, ALU.add)
                    for e in range(NE):
                        b = e % 2
                        dve.wait_ge(silu_done, it * NE + (e + 1))
                        V.tensor_tensor(hact[:, b, :], sil[:, b, :], ps[:, b, P:2 * P], ALU.mult
                                        ).then_inc(hact_done, 1)
                        if e == QUAD:
                            add_quad(it, 0)
                        dve.wait_ge(y_psum, it * NE + (e + 1))
                        r0 = CAP * (e % QUAD)
                        for c in (0, 1):
                            last = V.tensor_copy(yq[r0:r0 + CAP, e // QUAD, 256 * c:256 * (c + 1)],
                                                 ps[CAP * c:CAP * (c + 1), 2 + b, 0:256])
                        last.then_inc(y_dve, 1)
                    add_quad(it, 1)

                return passes(dve, layer, before, group)

            n1 = moe(0, 0)
            its = dve.snap(n1 * NG)

            store_transposed(2, [(2, xTkv), (3, xT)])

            def rope(dst, src, tmp, t, nh):
                hd = DH // 2
                for o, i, c0, c in ((dst, src, C_COS, slice(0, DH)),
                                    (tmp[:, :, 0:hd], src[:, :, hd:DH], C_SIN, slice(0, hd)),
                                    (tmp[:, :, hd:DH], src[:, :, 0:hd], C_SIN, slice(hd, DH))):
                    angles = cst[:, c0 + DH * t + c.start:c0 + DH * t + c.stop]
                    last = V.scalar_tensor_tensor(out=o, in0=i, scalar=ss[:, 2, t:t + 1],
                                                  in1=bc(angles.unsqueeze(1), 1, nh),
                                                  op0=ALU.mult, op1=ALU.mult)
                return last

            def rope_q(i):
                dve.wait_ge(q_psum, i + 1)
                if i >= 2:
                    dve.wait_ge(rope_done, i - 1)
                rope(ropes[:, i % 2, 0, :].rearrange("p (h d) -> p h d", h=8),
                     ps[:, 6 + i % 2, :].rearrange("p (h d) -> p h d", h=8),
                     ropes[:, i % 2, 1, :].rearrange("p (h d) -> p h d", h=8), i // 2, 8
                     ).then_inc(rope_dve, 1)

            def store_q(i):
                dve.wait_ge(qt_psum, i + 1)
                t, m0 = i // 2, 4 * (i % 2)
                V.tensor_scalar(qbd[DH:P, m0:m0 + 4, 2 * t:2 * t + 2, 1, :],
                                ps[DH:P, i, :].rearrange("p (m c q) -> p m c q", m=4, c=2),
                                SCALE, None, ALU.mult).then_inc(qt_dve, 1)

            def scored(c):
                b = 2 - 2 * (c % 2)
                w = CHUNK if c == 0 else 2 * CHUNK
                return ps[:, b:b + 2, :].rearrange("p x (m k) -> p (x m) k", m=4)[:, :, 0:w], w

            def shift(c):
                b = c % 2
                sc, w = scored(c)
                dve.wait_ge(s_psum, c + 1)
                link(V.tensor_reduce(mxB[:, b, :], sc, AX.X, ALU.max))
                link(V.tensor_tensor(mxB[:, b, :], mxB[:, b, :], sinks[:, :], ALU.max))
                if c >= 2:
                    dve.wait_ge(pt_psum, c - 1)
                else:
                    dve.wait_ge(rope_done, 3 + c)
                V.tensor_tensor(esB[:, b, :], sinks[:, :], mxB[:, b, :], ALU.subtract)
                V.tensor_tensor(pB[:, b, :, 0:w], sc, bc(mxB[:, b, :].unsqueeze(2), 2, w),
                                ALU.subtract).then_inc(shifted, 1)

            def normalise(c):
                b = c % 2
                _, w = scored(c)
                dve.wait_ge(p_exp, c + 1)
                link(V.tensor_reduce(mxB[:, b, :], pB[:, b, :, 0:w], AX.X, ALU.add))
                link(V.tensor_tensor(mxB[:, b, :], mxB[:, b, :], esB[:, b, :], ALU.add))
                link(V.reciprocal(mxB[:, b, :], mxB[:, b, :]))
                V.tensor_tensor(pB[:, b, :, 0:w], pB[:, b, :, 0:w],
                                bc(mxB[:, b, :].unsqueeze(2), 2, w), ALU.mult).then_inc(p_done, 1)

            def store_o(c):
                dve.wait_ge(ob_psum, c + 1)
                V.tensor_copy(oT[:, :, CHUNK * c:CHUNK * (c + 1)],
                              ps[:, 6, :].rearrange("p (m q) -> p m q", m=PAIRS)).then_inc(ob_done, 1)

            kvt = ps[:, 4, :].rearrange("p (t n) -> p t n", t=T)
            for a in range(2):
                V.tensor_copy(sinks[DH * a:DH * (a + 1), :],
                              sink16[DH * a:DH * (a + 1), :].rearrange("p (m a) -> p m a", a=2)[:, :, a])
            dve.wait_ge(rstd_done, 3)
            dve.wait_ge(kv_psum, 1)
            for t in range(T):
                ka, kb = (ropes[:, 0, r, 128 * t:128 * (t + 1)].rearrange("p (h d) -> p h d", h=KVH)
                          for r in range(2))
                link(rope(ka, kvt[:, t, 0:P].rearrange("p (h d) -> p h d", h=KVH), kb, t, KVH))
                for a in range(2):
                    last = V.tensor_tensor(k2[:, t, :, a, :], ka, kb, ALU.add)
            for r, win, r_in, t in ((slice(0, P), 0, slice(0, P), 0), (slice(0, P), 2, slice(0, P), 1),
                                    (slice(0, DH), 1, slice(DH, P), 0), (slice(DH, P), 1, slice(0, DH), 1)):
                last = V.tensor_scalar(vwin[r, win, :], kvt[r_in, t, P:2 * P], ss[r_in, 2, t:t + 1], None,
                                       ALU.mult)
            last.then_inc(kv_done, 1)
            dve.wait_ge(kv_done, 1)
            rope_q(0)
            rope_q(1)
            dve.wait_ge(kt_psum, 1)
            V.tensor_copy(kdup.rearrange("p h k -> p (h k)"), ps[:, 5, :]).then_inc(kt_done, 1)
            rope_q(2)
            dve.wait_ge(zeroed, 2)
            store_q(0)
            store_q(1)
            dve.wait_ge(rope_done, 3)
            V.memset(pB[:, 0, :, CHUNK:2 * CHUNK], 0.0)
            shift(0)
            normalise(0)
            rope_q(3)
            shift(1)
            store_q(2)
            store_q(3)
            store_o(0)
            normalise(1)
            shift(2)
            store_o(1)
            normalise(2)
            shift(3)
            normalise(3)
            add_attention(1, 0)
            store_o(2)
            add_attention(1, 1)
            store_o(3)
            add_attention(1, 2)
            add_attention(1, 3)
            moe(1, its)
            dve.wait_ge(rstd_done, 5)
            dve.wait_ge(fgain_in, 16)
            for t in range(T):
                V.scalar_tensor_tensor(out=xn[:, t, :], in0=h[:, t, :], scalar=ss[:, 2, t:t + 1],
                                       in1=fgain, op0=ALU.mult, op1=ALU.mult).then_inc(out_done, 1)

        @block.tensor
        def _(pe):
            MM = nc.tensor.matmul

            def transpose_rows(n, its=None):
                src = xn if n == 0 else h
                for t in range(T):
                    if n == 0:
                        pe.wait_ge(xn_done, t + 1)
                    else:
                        rows_stand(pe, n, t, its)
                    for k in range(KD):
                        last = nc.tensor.transpose(ps[:, 2 * t + k // 4, P * (k % 4):P * (k % 4 + 1)],
                                                   src[:, t, k::KD], ident)
                    last.then_inc(xt_psum, 1)
                pe.wait_ge(xt_act, T * (n + 1))
                pe.wait_ge(xt_dve, T * (n + 1))

            pe.wait_ge(const_in, 32)
            transpose_rows(0)
            for i in range(4):
                t, half = i % 2, i // 2
                s = SEQ_A + half
                wait_slot(pe, s)
                wv = slot(s).rearrange("p (k n) -> p k n", k=KD)
                for k in range(KD):
                    last = MM(ps[:, 4 + i, :], xT[:, k, P * t:P * (t + 1)], wv[:, k, :],
                              start=k == 0, stop=k == KD - 1)
                last.then_inc(v_psum, 1)

            def project_out(layer, i, seq, its, m0=0, m1=KD):
                t, half = i // 2, i % 2
                if m0 == 0:
                    wait_slot(pe, seq + half, its)
                w = slot(seq + half).rearrange("p (m n) -> p m n", m=KD)
                for m in range(m0, m1):
                    last = MM(ps[:, WO_BANKS[layer][i], :], oT[:, m, P * t:P * (t + 1)], w[:, m, :],
                              start=m == 0, stop=m == KD - 1)
                if m1 == KD:
                    last.then_inc(wo_psum, 1)

            for i in range(PAIRS + 3):
                if i < PAIRS:
                    m = i
                    s = SEQ_A + 2 + m // 2
                    wait_slot(pe, s)
                    if m >= 2:
                        pe.wait_ge(qk_done, m - 1)
                    w = slot(s).rearrange("p (k n) -> p k n", k=KD)
                    for j in range(2):
                        for k in range(KD):
                            c0 = 256 * j + P * (m % 2)
                            last = MM(ps[:, m % 2, SEQ * j:SEQ * (j + 1)], w[:, k, c0:c0 + P], xT[:, k, :],
                                      start=k == 0, stop=k == KD - 1)
                    last.then_inc(qk_psum, 1)
                if 0 <= i - 1 < PAIRS:
                    m = i - 1
                    b = m % 2
                    pe.wait_ge(qk_done, m + 1)
                    if m < 2:
                        pe.wait_ge(v_done, 2 * b + 2 if b == 0 else 4)
                    else:
                        pe.wait_ge(arg_done, m - 1)
                    for a in range(2):
                        z = ps[:, 2 + 2 * b + a, :]
                        MM(z[:, 0:SEQ], kz[:, b, a, 0:P], qT[:, b, :], start=True, stop=False,
                           skip_group_check=True)
                        last = MM(z[:, SEQ:SEQ + P], kz[:, b, a, P:SEQ], qT[:, b, P:SEQ], start=False,
                                  stop=False, skip_group_check=True)
                    last.then_inc(z_psum, 1)
                if 0 <= i - 2 < PAIRS:
                    m = i - 2
                    b = m % 2
                    pe.wait_ge(sp_done, m + 1)
                    for a in range(2):
                        z = ps[:, 2 + 2 * b + a, :]
                        s0 = sp[:, b, a, :]
                        MM(z[:, SEQ:SEQ + P], ntri, s0[:, SEQ:SEQ + P], start=False, stop=False,
                           skip_group_check=True)
                        MM(z[:, 0:SEQ], ntri, s0[:, 0:SEQ], start=False, stop=False, skip_group_check=True)
                        last = MM(z[:, P:SEQ], nones, s0[:, SEQ:SEQ + P], start=False, stop=True,
                                  skip_group_check=True)
                    last.then_inc(tail_psum, 1)
                if 0 <= i - 3 < PAIRS:
                    m = i - 3
                    b = m % 2
                    pe.wait_ge(w_done, m + 1)
                    pe.wait_ge(v_done, 4)
                    if m >= 2:
                        pe.wait_ge(o_done, m - 1)
                    for kt in range(2):
                        for a in range(2):
                            hd = 2 * m + a
                            last = MM(ps[DH * a:DH * (a + 1), 6 + b, P * kt:SEQ],
                                      v_rows[:, kt, DH * hd:DH * (hd + 1)],
                                      wA[:, b, a, SEQ * kt:SEQ if kt == 0 else SEQ + P],
                                      start=kt == 0, stop=kt == 1, skip_group_check=True)
                    last.then_inc(o_psum, 1)

                if i in (PAIRS, PAIRS + 1):
                    pe.wait_ge(o_done, PAIRS - 3)
                    project_out(0, i - PAIRS, SEQ_A + 6, 0, 0, PAIRS - 3)

            pe.wait_ge(o_done, PAIRS)
            for i in range(4):
                project_out(0, i, SEQ_A + 6, 0, PAIRS - 3 if i < 2 else 0)

            def moe(layer, before):
                seq = SEQ_M[layer]
                transpose_rows(1 + 2 * layer)
                pe.wait_ge(prepared, 1)
                for t in range(T):
                    for k in range(KD):
                        last = MM(ps[:, 4, 64 * t:64 * t + NG + EXP], xT[:, k, P * t:P * (t + 1)],
                                  wr[:, layer, k, :], start=k == 0, stop=k == KD - 1)
                last.then_inc(lg_psum, 1)
                pe.wait_ge(member_done, layer + 1)
                for t in range(T + 1):
                    for u in range(min(t + 1, T)):
                        last = MM(ps[:, 5, EXP * t:EXP * (t + 1)], counting[:, 0 if u == t else 1, :],
                                  member[:, u, :], start=u == 0, stop=u == min(t, T - 1))
                last.then_inc(rank_psum, 1)

                def combine(it, q):
                    pe.wait_ge(y_act, it * NE + (QUAD * (q + 1) + 1))
                    pe.wait_ge(y_dve, it * NE + (QUAD * (q + 1) + 1))
                    if q == 0:
                        pe.wait_ge(selt_done, it + 1)
                    for i in range(4):
                        t, half = i // 2, i % 2
                        if i >= 2:
                            pe.wait_ge(added[0], it * 4 + (2 * q + half + 1))
                        elif q == 1:
                            pe.wait_ge(added[1], it * 4 + (half + 1))
                        MM(ps[:, 6 + i % 2, :], selT[:, q, t, :], yq[:, q, 512 * half:512 * (half + 1)],
                           start=True, stop=True).then_inc(comb_psum, 1)

                def group(g, it):
                    pe.wait_ge(selg_done, it + 1)
                    pe.wait_ge(xn_done, T * (layer + 2))
                    for k in range(KD):
                        if k >= 2:
                            pe.wait_ge(xg_done, it * KD + (k - 1))
                        for t in range(T):
                            last = MM(ps[:, 6 + k % 2, 0:NE * CAP], xn[:, t, k::KD], selg[:, t, :],
                                      start=t == 0, stop=t == T - 1)
                        last.then_inc(xg_psum, 1)
                    pe.wait_ge(selw_done, it + 1)
                    for q in range(2):
                        for t in range(T):
                            last = nc.tensor.transpose(ps[:, 5, P * (2 * q + t):P * (2 * q + t + 1)],
                                                       selw[:, t, P * q:P * (q + 1)], ident)
                    last.then_inc(selt_psum, 1)
                    pe.wait_ge(xg_done, it * KD + KD)
                    for e in range(NE):
                        b = e % 2
                        s = seq + 3 * e
                        for half in range(2):
                            wait_slot(pe, s + half, it)
                            w = slot(s + half).rearrange("p (u k f) -> p u k f", u=2, k=4)
                            for k in range(4):
                                for j in range(4):
                                    kk = 4 * half + k
                                    last = MM(ps[CAP * j:CAP * (j + 1), b, 0:2 * P].rearrange(
                                                  "p (u f) -> p u f", u=2),
                                              xg[:, kk, CAP * e:CAP * (e + 1)],
                                              w[:, :, k, P * j:P * (j + 1)],
                                              start=kk == 0, stop=kk == KD - 1, skip_group_check=True)
                            last.then_inc(gu_psum if half else gu_half, 1)
                        if e == QUAD:
                            combine(it, 0)
                        pe.wait_ge(hact_done, it * NE + (e + 1))
                        nc.tensor.transpose(ps[:, 4, 0:P], hact[:, b, :], ident).then_inc(ht_psum, 1)
                        pe.wait_ge(ht_done, it * NE + (e + 1))
                        pe.wait_ge(y_act, it * NE + (e + 1))
                        pe.wait_ge(y_dve, it * NE + (e + 1))
                        wait_slot(pe, s + 2, it)
                        w = slot(s + 2).rearrange("p (j n) -> p j n", j=4)
                        for j in range(4):
                            for c in range(4):
                                last = MM(ps[CAP * c:CAP * (c + 1), 2 + b, 0:256],
                                          hT[:, b, CAP * j:CAP * (j + 1)],
                                          w[:, j, 256 * c:256 * (c + 1)],
                                          start=j == 0, stop=j == 3, skip_group_check=True)
                        last.then_inc(y_psum, 1)
                    combine(it, 1)

                return passes(pe, layer, before, group)

            n1 = moe(0, 0)
            its = pe.snap(n1 * NG)

            transpose_rows(2, its)

            def project_q(i):
                t, half = i // 2, i % 2
                s = SEQ_B + 1 + half
                wait_slot(pe, s, its)
                if i >= 2:
                    pe.wait_ge(rope_dve, i - 1)
                w = slot(s).rearrange("p (k n) -> p k n", k=KD)
                for k in range(KD):
                    last = MM(ps[:, 6 + i % 2, :], xT[:, k, P * t:P * (t + 1)], w[:, k, :],
                              start=k == 0, stop=k == KD - 1)
                last.then_inc(q_psum, 1)

            def transpose_q(t):
                pe.wait_ge(rope_done, 2 * (t + 1))
                if t == 1:
                    pe.wait_ge(shifted, 1)
                for half in range(2):
                    for m in range(4):
                        mm = 4 * half + m
                        last = nc.tensor.transpose(ps[:, 2 * t + half, P * m:P * (m + 1)],
                                                   q_rows[:, t, P * mm:P * (mm + 1)], ident)
                    last.then_inc(qt_psum, 1)

            def scores(c):
                b = 2 - 2 * (c % 2)
                if c < 3:
                    pe.wait_ge(qt_act, 2 * (c // 2 + 1))
                    pe.wait_ge(qt_dve, 2 * (c // 2 + 1))
                else:
                    pe.wait_ge(shifted, 2)
                k0 = max(0, CHUNK * (c - 1))
                for m in range(PAIRS):
                    last = MM(ps[:, b + m // 4, P * (m % 4):P * (m % 4 + 1)],
                              qbd[:, m, c, :, :].rearrange("p a q -> p (a q)"),
                              kdup[:, m // (PAIRS // KVH), k0:k0 + P], start=True, stop=True)
                last.then_inc(s_psum, 1)

            def transpose_p(c):
                pe.wait_ge(p_done, c + 1)
                if c >= 1:
                    pe.wait_ge(pt_done, c)
                for m in range(PAIRS):
                    last = nc.tensor.transpose(ps[:, 4 + m // 4, P * (m % 4):P * (m % 4 + 1)],
                                               pB[:, c % 2, m, :], ident)
                last.then_inc(pt_psum, 1)

            def weigh_v(c):
                pe.wait_ge(pt_done, c + 1)
                if c >= 1:
                    pe.wait_ge(ob_done, c)
                else:
                    pe.wait_ge(rope_dve, 3)
                win = max(0, c - 1)
                for hk in range(KVH):
                    for a in range(2):
                        last = MM(ps[DH * a:DH * (a + 1), 6, 256 * hk:256 * (hk + 1)].rearrange(
                                      "p (m q) -> p m q", m=4),
                                  vwin[:, win, DH * hk:DH * (hk + 1)],
                                  pT[:, 4 * hk:4 * hk + 4, DH * a:DH * (a + 1)],
                                  start=True, stop=True, skip_group_check=True)
                last.then_inc(ob_psum, 1)

            wait_slot(pe, SEQ_B, its)
            w = slot(SEQ_B)[:, 0:KD * 256].rearrange("p (k n) -> p k n", k=KD)
            for t in range(T):
                for k in range(KD):
                    last = MM(ps[:, 4, 256 * t:256 * (t + 1)], xTkv[:, k, P * t:P * (t + 1)], w[:, k, :],
                              start=k == 0, stop=k == KD - 1)
            last.then_inc(kv_psum, 1)
            project_q(0)
            project_q(1)
            pe.wait_ge(kv_done, 1)
            for hk in range(KVH):
                for t in range(T):
                    c0 = SEQ * hk + P * t
                    last = nc.tensor.transpose(ps[:, 5, c0:c0 + P],
                                               k2[:, t, hk, :, :].rearrange("p a d -> p (a d)"), ident)
            last.then_inc(kt_psum, 1)
            project_q(2)
            transpose_q(0)
            pe.wait_ge(kt_done, 1)
            scores(0)
            project_q(3)
            scores(1)
            transpose_p(0)
            transpose_q(1)
            weigh_v(0)
            scores(2)
            transpose_p(1)
            weigh_v(1)
            scores(3)
            pe.wait_ge(ob_done, 2)
            pe.wait_ge(rope_dve, 4)
            project_out(1, 0, SEQ_B + 3, its)
            transpose_p(2)
            weigh_v(2)
            pe.wait_ge(shifted, 3)
            project_out(1, 1, SEQ_B + 3, its)
            transpose_p(3)
            weigh_v(3)
            pe.wait_ge(ob_done, 4)
            project_out(1, 2, SEQ_B + 3, its)
            pe.wait_ge(h_done, 4 + 1)
            project_out(1, 3, SEQ_B + 3, its)
            moe(1, its)


N_PARAMS = 4 + 8 + 1

_INS = ["x", "a_norm", "a_w_qkv", "a_w_o", "kv_norm", "kv_w", "b_norm", "b_w_q", "b_sinks", "b_w_o",
        "ffn_norm", "moe_w_group", "moe_b_group", "moe_w_router", "moe_b_router", "moe_w_gate",
        "moe_w_up", "moe_w_down", "final_norm"]


def kernel(**inputs):
    import concourse.bacc as bacc
    from concourse.bass_utils import run_bass_kernel_spmd

    nc = bacc.Bacc("TRN2", target_bir_lowering=False, num_devices=1)
    arrays = {f"in_{n}": np.ascontiguousarray(inputs[n]) for n in _INS}
    arrays["in_consts"] = shape_constants()
    args = [nc.dram_tensor(n, a.shape, mybir.dt.from_np(a.dtype), kind="ExternalInput").ap()
            for n, a in arrays.items()]
    args.append(nc.dram_tensor("out_0", (1, SEQ, D), F32, kind="ExternalOutput").ap())
    build(nc, *args)
    r = run_bass_kernel_spmd(nc, [arrays], core_ids=[0])
    return r.results[0]["out_0"]
```

```python
from contextlib import ExitStack

import numpy as np
import concourse.bass as bass
from concourse import mybir

F32 = mybir.dt.float32
BF16 = mybir.dt.bfloat16
I32 = mybir.dt.int32
U32 = mybir.dt.uint32
ALU = mybir.AluOpType
ACT = mybir.ActivationFunctionType
AX = mybir.AxisListType

P = 128
SEQ, D = 256, 1024
T = SEQ // P
KD = D // P
DH = 64
HEADS = D // DH
PAIRS = HEADS // 2
KVH = 2
CHUNK = 64
NCH = SEQ // CHUNK
NG, NE = 4, 8
EXP = NG * NE
FF = D // 2
CAP = 32
QUAD = P // CAP
RING = 9
SLOT = 4096
SLOTS_GROUP = 3 * NE
N_A, N_B = 8, 5
SCRATCH = 4992
EPS = 1e-6
FAR = 10000.0
SCALE = DH ** -0.5

C_ID, C_NTRI, C_NONE, C_STRICT, C_CAP = (P * i for i in range(5))
C_MASK = C_STRICT
C_COS = 5 * P
C_SIN = C_COS + T * DH
C_IOTA = C_SIN + T * DH
C_THR = C_IOTA + CAP
N_THR = SEQ // CAP - 1
C_POW = C_THR + 8
N_CONST = C_POW + 8


def bc(ap, axis, n):
    shape = list(ap.shape)
    assert shape[axis] == 1
    shape[axis] = n
    return ap.broadcast_to(shape)


def shape_constants():
    c = np.zeros((P, N_CONST), np.float32)
    row, col = np.arange(P)[:, None], np.arange(P)[None, :]
    c[:, C_ID:C_ID + P] = row == col
    c[:, C_NTRI:C_NTRI + P] = -1.0 * (row >= col)
    c[:, C_NONE:C_NONE + P] = -1.0
    c[:, C_STRICT:C_STRICT + P] = row < col
    c[:, C_CAP:C_CAP + P] = np.where(row < col, 0.0, -FAR)
    half = DH // 2
    inv = np.float32(10000.0) ** (-np.arange(half, dtype=np.float32) / np.float32(half))
    for t in range(T):
        ang = (np.arange(P) + P * t).astype(np.float32)[:, None] * inv[None, :].astype(np.float32)
        cos, sin = np.cos(ang), np.sin(ang)
        c[:, C_COS + DH * t:C_COS + DH * (t + 1)] = np.concatenate([cos, cos], 1)
        c[:, C_SIN + DH * t:C_SIN + DH * (t + 1)] = np.concatenate([-sin, sin], 1)
    c[:, C_IOTA:C_IOTA + CAP] = np.arange(CAP)
    c[:, C_THR:C_THR + N_THR] = CAP * (1 + np.arange(N_THR))
    c[:, C_POW:C_POW + T] = -0.5
    return c


def build(nc, x, a_norm, a_w_qkv, a_w_o, kv_norm, kv_w, b_norm, b_w_q, b_sinks, b_w_o, ffn_norm,
          moe_w_group, moe_b_group, moe_w_router, moe_b_router, moe_w_gate, moe_w_up, moe_w_down,
          final_norm, consts, out):
    ctx = ExitStack()
    with ctx:
        def sb(name, shape, dt=F32):
            return ctx.enter_context(nc.sbuf_tensor(name, shape, dt))

        def sem(name):
            return ctx.enter_context(nc.semaphore(name))

        ring = sb("ring", [P, RING, SLOT])
        h = sb("h", [P, T, D])
        xn = sb("xn", [P, T, D])
        xT = sb("xT", [P, KD, SEQ])
        oT = sb("oT", [P, KD, SEQ])
        scr = sb("scr", [P, SCRATCH])
        cst = sb("cst", [P, N_CONST])
        gain = sb("gain", [P, 5, KD])
        wr_in = sb("wr_in", [P, 2, KD * (NG + EXP)])
        wr = sb("wr", [P, 2, KD, NG + EXP])
        rbias = sb("rbias", [P, 2, NG + EXP])
        sink16 = sb("sink16", [P, HEADS])
        sinks = sb("sinks", [P, PAIRS])
        ss = sb("ss", [P, 3, T])
        counting = sb("counting", [P, 2, P], BF16)
        member = sb("member", [P, T, EXP], BF16)
        small = sb("small", [P, 512])
        idx8 = sb("idx8", [P, 2, T, 8], U32)
        npass = sb("npass", [P, 2], I32)
        tokw = sb("tokw", [P, T, EXP])
        rank = sb("rank", [P, T, EXP])

        ps = ctx.enter_context(nc.psum_tensor("ps", [P, 8, 512], F32))

        ident = cst[:, C_ID:C_ID + P]
        ntri = cst[:, C_NTRI:C_NTRI + P]
        nones = cst[:, C_NONE:C_NONE + P]
        strict = cst[:, C_STRICT:C_STRICT + P]
        maskc = cst[:, C_MASK:C_MASK + P]
        capc = cst[:, C_CAP:C_CAP + P]
        iota = cst[:, C_IOTA:C_IOTA + CAP]
        v_rows = q_rows = xn
        xTkv = oT
        xg = xT

        at = [0]

        def cut(n):
            at[0] += n
            assert at[0] <= SCRATCH
            return scr[:, at[0] - n:at[0]]

        qT = cut(2 * SEQ).rearrange("p (b q) -> p b q", b=2)
        kz = cut(4 * SEQ).rearrange("p (b a k) -> p b a k", b=2, a=2)
        za = cut(4 * 3 * P).rearrange("p (b a n) -> p b a n", b=2, a=2)
        sp = za
        wA = cut(4 * 3 * P).rearrange("p (b a n) -> p b a n", b=2, a=2)
        at[0] = 0
        kdup = cut(KVH * SEQ).rearrange("p (h k) -> p h k", h=KVH)
        vwin = cut(3 * P).rearrange("p (w n) -> p w n", w=3)
        pB = cut(2 * PAIRS * P).rearrange("p (b m k) -> p b m k", b=2, m=PAIRS)
        qbd = cut(PAIRS * 2 * P).rearrange("p (m c a q) -> p m c a q", m=PAIRS, c=2, a=2)
        kr = pB[:, 0, 0:4, :].rearrange("p m k -> p (m k)").rearrange("p (r n) -> p r n", r=2)
        k2 = oT[:, 0:2, :].rearrange("p t n -> p (t n)").rearrange(
            "p (t h a d) -> p t h a d", t=T, h=KVH, a=2)
        ropes = oT[:, 2:6, :].rearrange("p t n -> p (t n)").rearrange("p (b n) -> p b n", b=2)
        pT = xT[:, :, :].rearrange("p k n -> p (k n)").rearrange(
            "p (b m n) -> p b m n", b=2, m=PAIRS)
        at[0] = 0
        selg = cut(T * NE * CAP).rearrange("p (t n) -> p t n", t=T)
        selw = cut(T * NE * CAP).rearrange("p (t n) -> p t n", t=T)
        selT = cut(2 * T * P).rearrange("p (q t n) -> p q t n", q=2, t=T)
        sil = cut(2 * P).rearrange("p (b n) -> p b n", b=2)
        hact = cut(2 * P).rearrange("p (b n) -> p b n", b=2)
        hT = cut(2 * P).rearrange("p (b n) -> p b n", b=2)
        yq = cut(2 * D).rearrange("p (q n) -> p q n", q=2)
        fgain = oT[:, 0:4, :].rearrange("p k n -> p (k n)")

        so = [0]

        def tiny(n):
            so[0] += n
            assert so[0] <= 512
            return small[:, so[0] - n:so[0]]

        logit = tiny(T * (NG + EXP)).rearrange("p (t n) -> p t n", t=T)
        gpad = tiny(T * 8).rearrange("p (t n) -> p t n", t=T)
        gtop8 = tiny(T * 8).rearrange("p (t n) -> p t n", t=T)
        etop8 = tiny(T * 8).rearrange("p (t n) -> p t n", t=T)
        esel = tiny(T * 8).rearrange("p (t n) -> p t n", t=T)
        gidx = tiny(T).rearrange("p (t n) -> p t n", t=T)
        eidx = tiny(2 * T).rearrange("p (t n) -> p t n", t=T)
        goh = tiny(T * NG).rearrange("p (t n) -> p t n", t=T)
        gexp = tiny(T * NG).rearrange("p (t n) -> p t n", t=T)
        gsum = tiny(T)
        oh = tiny(2 * T * NE).rearrange("p (r t n) -> p r t n", r=2, t=T)
        prod = tiny(T * EXP).rearrange("p (t g e) -> p t g e", t=T, g=NG)
        e2 = tiny(T)
        w12 = tiny(2 * T).rearrange("p (r t) -> p r t", r=2)
        wsum = tiny(T * NE).rearrange("p (t n) -> p t n", t=T)
        msum = tiny(T * NE).rearrange("p (t n) -> p t n", t=T)
        cnt = tiny(2)
        thr = tiny(8)
        mxB = tiny(2 * PAIRS).rearrange("p (b m) -> p b m", b=2)
        nmxB = tiny(2 * PAIRS).rearrange("p (b m) -> p b m", b=2)
        sumB = tiny(2 * PAIRS).rearrange("p (b m) -> p b m", b=2)
        esB = tiny(2 * PAIRS).rearrange("p (b m) -> p b m", b=2)

        landed = [sem(f"landed{i}") for i in range(RING)]
        freed = sem("freed")
        x_in = [sem(f"x_in{t}") for t in range(T)]
        const_in = sem("const_in")
        params_in = sem("params_in")
        prepared = sem("prepared")
        fgain_in = sem("fgain_in")
        zeroed = sem("zeroed")
        squared = sem("squared")
        var_done = sem("var_done")
        rstd_done = sem("rstd_done")
        xn_done = sem("xn_done")
        out_done = sem("out_done")
        xt_psum = sem("xt_psum")
        xt_act = sem("xt_act")
        xt_dve = sem("xt_dve")
        vchain = sem("vchain")
        v_psum = sem("v_psum")
        v_done = sem("v_done")
        qk_psum = sem("qk_psum")
        qk_done = sem("qk_done")
        z_psum = sem("z_psum")
        zabs_done = sem("zabs_done")
        zexp_done = sem("zexp_done")
        zln_done = sem("zln_done")
        sp_done = sem("sp_done")
        tail_psum = sem("tail_psum")
        arg_done = sem("arg_done")
        w_done = sem("w_done")
        o_psum = sem("o_psum")
        o_done = sem("o_done")
        wo_psum = sem("wo_psum")
        h_done = sem("h_done")
        kv_psum = sem("kv_psum")
        kv_done = sem("kv_done")
        kt_psum = sem("kt_psum")
        kt_done = sem("kt_done")
        q_psum = sem("q_psum")
        rope_dve = sem("rope_dve")
        rope_done = sem("rope_done")
        qt_psum = sem("qt_psum")
        qt_act = sem("qt_act")
        qt_dve = sem("qt_dve")
        s_psum = sem("s_psum")
        max_done = sem("max_done")
        p_exp = sem("p_exp")
        p_done = sem("p_done")
        pt_psum = sem("pt_psum")
        pt_done = sem("pt_done")
        ob_psum = sem("ob_psum")
        ob_done = sem("ob_done")
        lg_psum = sem("lg_psum")
        gsub_done = sem("gsub_done")
        gexp_done = sem("gexp_done")
        member_done = sem("member_done")
        rank_psum = sem("rank_psum")
        routed = sem("routed")
        selg_done = sem("selg_done")
        selw_done = sem("selw_done")
        selt_psum = sem("selt_psum")
        selt_done = sem("selt_done")
        xg_psum = sem("xg_psum")
        xg_done = sem("xg_done")
        gu_half = sem("gu_half")
        gu_psum = sem("gu_psum")
        silu_done = sem("silu_done")
        hact_done = sem("hact_done")
        ht_psum = sem("ht_psum")
        ht_done = sem("ht_done")
        y_psum = sem("y_psum")
        y_act = sem("y_act")
        y_dve = sem("y_dve")
        comb_psum = sem("comb_psum")
        added = [sem(f"added{t}") for t in range(T)]
        counted = sem("counted")
        stored = sem("stored")

        block = ctx.enter_context(nc.Block())

        WO_BANKS = ((0, 1, 2, 3), (7, 2, 3, 7))

        FIRST = (0, 2)

        def slot_a(i):
            return i

        def slot_b(i):
            return (6 + i) % RING

        def slot_m(layer, s):
            return (s + FIRST[layer]) % RING

        PER = [[sum(slot_m(l, s) == b for s in range(SLOTS_GROUP)) for b in range(RING)]
               for l in range(2)]
        IN_A = [sum(slot_a(i) == b for i in range(N_A)) for b in range(RING)]
        IN_B = [sum(slot_b(i) == b for i in range(N_B)) for b in range(RING)]

        def slot(b):
            return ring[:, b, :]

        def wait_a(eng, i):
            eng.wait_ge(landed[slot_a(i)], 32)

        def wait_b(eng, i, its):
            b = slot_b(i)
            eng.wait_ge(landed[b], its * (32 * PER[0][b]) + 32 * (IN_A[b] + 1))

        def wait_m(eng, layer, s, its, lit):
            b = slot_m(layer, s)
            here = 32 * (IN_A[b] + layer * IN_B[b] + s // RING + 1)
            if layer == 0:
                eng.wait_ge(landed[b], lit * (32 * PER[0][b]) + here)
            else:
                eng.wait_ge(landed[b], its * (32 * PER[0][b]) + lit * (32 * PER[1][b]) + here)

        def rows_stand(eng, n, t, its=None):
            if n == 0:
                eng.wait_ge(x_in[t], 16)
            elif n % 2:
                eng.wait_ge(h_done, 4 * (n // 2) + 2 * (t + 1))
            else:
                eng.wait_ge(added[t], its * 4)

        def passes(eng, layer, before, group, peel=False):
            if peel:
                group(0, before, 0)
            with eng.Fori(1 if peel else 0, NG) as g:
                group(g, eng.snap(g + before), g)
            eng.wait_ge(routed, layer + 1)
            n = eng.value_load(npass[0:1, layer:layer + 1], min_val=1, max_val=SEQ // CAP)
            with eng.If(n > 1):
                with eng.Fori(1, n) as r:
                    with eng.Fori(0, NG) as g:
                        lit = eng.snap(r * NG + g)
                        group(g, eng.snap(lit + before), lit)
            with eng.Else():
                eng.nop()
            return n

        @block.sync
        def _(sp_):
            def load(b, parts, its=0, used=0):
                if isinstance(its, int):
                    if its * SLOTS_GROUP + used:
                        sp_.wait_ge(freed, its * SLOTS_GROUP + used)
                else:
                    sp_.wait_ge(freed, its * SLOTS_GROUP + used)
                for dst, src in parts:
                    sp_.dma_start(dst, src).then_inc(landed[b], 16)

            def by_k(s, w, c0, n):
                v = w.rearrange("(p k) n -> p k n", p=P)
                t = slot(s)[:, 0:KD * n].rearrange("p (k n) -> p k n", k=KD)
                return [(t[:, 4 * i:4 * i + 4, :], v[:, 4 * i:4 * i + 4, c0:c0 + n]) for i in range(2)]

            def by_m(s, w, c0, n):
                v = w.rearrange("(m p) n -> p m n", p=P)
                t = slot(s).rearrange("p (m n) -> p m n", m=KD)
                return [(t[:, 4 * i:4 * i + 4, :], v[:, 4 * i:4 * i + 4, c0:c0 + n]) for i in range(2)]

            for t in range(T):
                sp_.dma_start(h[:, t, :], x[0, P * t:P * (t + 1), :]).then_inc(x_in[t], 16)
            sp_.dma_start(cst[:, :], consts).then_inc(const_in, 16)
            sp_.dma_start(gain[:, 0, :], a_norm[0].rearrange("(p k) -> p k", p=P)).then_inc(const_in, 16)
            wq = a_w_qkv[0]
            for i in range(2):
                load(i, by_k(i, wq, 2 * D + 512 * i, 512))
            for i in range(4):
                v = wq.rearrange("(p k) n -> p k n", p=P)
                t = slot(2 + i).rearrange("p (k n) -> p k n", k=KD)
                load(2 + i, [(t[:, :, 256 * j:256 * (j + 1)],
                              v[:, :, D * j + 256 * i:D * j + 256 * (i + 1)]) for j in range(2)])
            for i in range(2):
                load(6 + i, by_m(6 + i, a_w_o[0], 512 * i, 512))

            pars = [(gain[:, 1 + i, :], g.rearrange("(p k) -> p k", p=P))
                    for i, g in enumerate((ffn_norm[0], kv_norm, b_norm[0], ffn_norm[1]))]
            for l in range(2):
                pars += [(wr_in[:, l, 0:KD * NG], moe_w_group[l].rearrange("(p k) g -> p (k g)", p=P)),
                         (wr_in[:, l, KD * NG:], moe_w_router[l].rearrange("(p k) g e -> p (k g e)", p=P)),
                         (rbias[:, l, 0:NG], bc(moe_b_group[l:l + 1, :], 0, P)),
                         (rbias[:, l, NG:], bc(moe_b_router[l:l + 1].rearrange("a g e -> a (g e)"), 0, P))]
            pars.append((sink16[:, :], bc(b_sinks[0:1, :], 0, P)))
            assert len(pars) == N_PARAMS
            for dst, src in pars:
                sp_.dma_start(dst, src).then_inc(params_in, 16)

            def load_group(layer, g, its, lit):
                def of(w, e):
                    return w[layer][bass.ds(g, 1), e].rearrange("a (p k) f -> (a p) k f", p=P)

                def used(s):
                    ahead = N_A + layer * N_B
                    if s >= RING:
                        return ahead + s - RING + 1
                    if isinstance(lit, int):
                        if layer == 0:
                            return s + 1 if s < N_A else 0
                        return ahead + s - RING + 1
                    return ahead + 1 - SLOTS_GROUP + max(
                        i for i in range(SLOTS_GROUP) if slot_m(layer, i) == slot_m(layer, s))

                for e in range(NE):
                    for half in range(2):
                        s = 3 * e + half
                        b = slot_m(layer, s)
                        t = slot(b).rearrange("p (u k f) -> p u k f", u=2, k=4)
                        load(b, [(t[:, u], of(w, e)[:, 4 * half:4 * half + 4, :])
                                 for u, w in enumerate((moe_w_gate, moe_w_up))], its, used(s))
                    s = 3 * e + 2
                    b = slot_m(layer, s)
                    t = slot(b).rearrange("p (j n) -> p j n", j=4)
                    wd = moe_w_down[layer][bass.ds(g, 1), e].rearrange("a (j p) n -> (a p) j n", p=P)
                    load(b, [(t[:, 2 * i:2 * i + 2, :], wd[:, 2 * i:2 * i + 2, :])
                             for i in range(2)], its, used(s))

            def load_layer(layer, before):
                return passes(sp_, layer, before,
                              lambda g, its, lit: load_group(layer, g, its, lit), peel=True)

            n1 = load_layer(0, 0)
            its = sp_.snap(n1 * NG)
            for i, parts in enumerate(
                    [by_k(slot_b(0), kv_w, 0, 256)]
                    + [by_k(slot_b(1 + i), b_w_q[0], 512 * i, 512) for i in range(2)]
                    + [by_m(slot_b(3 + i), b_w_o[0], 512 * i, 512) for i in range(2)]):
                load(slot_b(i), parts, its, N_A + i - RING + 1)
            load_layer(1, its)
            for t in range(T):
                sp_.wait_ge(out_done, t + 1)
                sp_.dma_start(out[0, P * t:P * (t + 1), :], xn[:, t, :]).then_inc(stored, 16)
            sp_.wait_ge(stored, 16 * T)

        @block.gpsimd
        def _(pool):
            nc.gpsimd.memset(kz[:, :, :, :], 0.0).then_inc(zeroed, 1)

            def norm(n):
                pool.wait_ge(squared, T * (n + 1))
                if n == 0:
                    pool.wait_ge(const_in, 32)
                nc.gpsimd.tensor_scalar(ss[:, 1, :], ss[:, 0, :], 1.0 / D, EPS, ALU.mult, ALU.add
                                        ).then_inc(var_done, 1)
                pool.wait_ge(var_done, n + 1)
                nc.gpsimd.tensor_tensor(ss[:, 2, :], ss[:, 1, :], cst[:, C_POW:C_POW + T], ALU.pow
                                        ).then_inc(rstd_done, 1)

            def free(done, count):
                pool.wait_ge(done, count)
                pool.sem_inc(freed, 1)

            def free_experts(layer, before):
                pool.wait_ge(counted, layer + 1)
                nc.gpsimd.tensor_copy(npass[:, layer:layer + 1], cnt[:, 1:2]).then_inc(routed, 1)

                def free_group(g, it, lit):
                    for e in range(NE):
                        for done in (gu_half, gu_psum, y_psum):
                            free(done, it * NE + (e + 1))

                return passes(pool, layer, before, free_group)

            norm(0)
            for i in range(2):
                free(v_psum, 2 * (i + 1))
            for i in range(4):
                free(qk_psum, 2 * (i + 1))
            pool.wait_ge(params_in, 16 * N_PARAMS)
            for l, gi in enumerate((1, 4)):
                for c0, n0, n in ((0, 0, NG), (KD * NG, NG, EXP)):
                    nc.gpsimd.tensor_tensor(
                        wr[:, l, :, n0:n0 + n],
                        wr_in[:, l, c0:c0 + KD * n].rearrange("p (k n) -> p k n", k=KD),
                        bc(gain[:, gi, :].unsqueeze(2), 2, n), ALU.mult)
            nc.gpsimd.tensor_copy(counting[:, 0, :], strict)
            nc.gpsimd.tensor_scalar(counting[:, 1, :], nones, -1.0, None, ALU.mult).then_inc(prepared, 1)
            for i in range(2):
                free(wo_psum, 3 + i)
            norm(1)
            n1 = free_experts(0, 0)
            norm(2)
            nc.gpsimd.memset(qbd.rearrange("p m c a q -> p (m c a q)"), 0.0).then_inc(zeroed, 1)
            free(kv_psum, 1)
            for i in range(4):
                t, half = i // 2, i % 2
                pool.wait_ge(rope_dve, i + 1)
                r = q_rows[:, t, 512 * half:512 * (half + 1)]
                nc.gpsimd.tensor_tensor(r, r, ropes[:, half, :], ALU.add).then_inc(rope_done, 1)
                if i == 1:
                    pool.wait_ge(kv_done, 1)
                    nc.gpsimd.memset(pB[:, 0, :, CHUNK:2 * CHUNK], 0.0).then_inc(zeroed, 1)
                if t == T - 1:
                    free(q_psum, i + 1)
            for i in range(2):
                free(wo_psum, 4 + 3 + i)
            norm(3)
            free_experts(1, pool.snap(n1 * NG))
            norm(4)

        @block.scalar
        def _(act):
            def norm_squares(n, its=None):
                for t in range(T):
                    rows_stand(act, n, t, its)
                    nc.scalar.activation(xn[:, t, :], h[:, t, :], ACT.Square,
                                         accum_out=ss[:, 0, t:t + 1]).then_inc(squared, 1)

            def store_transposed(n, gains):
                for t in range(T):
                    act.wait_ge(xt_psum, T * n + t + 1)
                    for gi, dst in gains:
                        src = ps[:, 2 * t, :].rearrange("p (k q) -> p k q", k=4)
                        if gi is None:
                            last = nc.scalar.activation(dst[:, 0:4, P * t:P * (t + 1)], src, ACT.Copy)
                            continue
                        for k in range(4):
                            last = nc.scalar.activation(dst[:, k, P * t:P * (t + 1)], src[:, k, :], ACT.Copy,
                                                        scale=gain[:, gi, k:k + 1])
                    last.then_inc(xt_act, 1)

            nc.scalar.memzero(idx8[:, 0, 0, 0:1]).then_inc(y_act, 1)

            norm_squares(0)
            act.wait_ge(const_in, 32)
            store_transposed(0, [(0, xT)])
            act.wait_ge(zeroed, 1)

            def qk_store(m):
                act.wait_ge(qk_psum, m + 1)
                b = m % 2
                if m >= 2:
                    act.wait_ge(z_psum, m - 1)
                nc.scalar.activation(qT[:, b, :], ps[:, b, 0:SEQ], ACT.Copy, scale=SCALE)
                for a in range(2):
                    r = slice(DH * a, DH * (a + 1))
                    last = nc.scalar.activation(kz[r, b, a, :], ps[r, b, SEQ:2 * SEQ], ACT.Copy)
                last.then_inc(qk_done, 1)

            for i in range(PAIRS + 2):
                if i < PAIRS:
                    qk_store(i)
                if 0 <= i - 1 < PAIRS:
                    m = i - 1
                    act.wait_ge(z_psum, m + 1)
                    if m >= 2:
                        act.wait_ge(tail_psum, m - 1)
                    nc.scalar.activation(za[:, m % 2, :, :],
                                         ps[:, 2 + 2 * (m % 2):4 + 2 * (m % 2), 0:384], ACT.Abs
                                         ).then_inc(zabs_done, 1)
                    act.wait_ge(zabs_done, m + 1)
                    nc.scalar.activation(za[:, m % 2, :, :], za[:, m % 2, :, :], ACT.Exp,
                                         scale=-1.0).then_inc(zexp_done, 1)
                if 0 <= i - 2 < PAIRS:
                    act.wait_ge(arg_done, i - 1)
                    nc.scalar.activation(wA[:, i % 2, :, :], wA[:, i % 2, :, :], ACT.Exp
                                         ).then_inc(w_done, 1)
                if 0 <= i - 1 < PAIRS:
                    act.wait_ge(zexp_done, m + 1)
                    nc.scalar.activation(za[:, m % 2, :, :], za[:, m % 2, :, :], ACT.Ln,
                                         bias=1.0).then_inc(zln_done, 1)

            def moe(layer, before):
                gi = 1 + 3 * layer
                norm_squares(1 + 2 * layer)
                store_transposed(1 + 2 * layer, [(None, xT)])
                act.wait_ge(rstd_done, 2 + 2 * layer)
                for t in range(T):
                    nc.scalar.activation(xn[:, t, :], h[:, t, :], ACT.Copy, scale=ss[:, 2, t:t + 1]
                                         ).then_inc(xn_done, 1)
                act.wait_ge(gsub_done, 2 * layer + 1)
                nc.scalar.activation(gexp[:, :, :], gexp[:, :, :], ACT.Exp).then_inc(gexp_done, 1)
                act.wait_ge(gsub_done, 2 * layer + 2)
                nc.scalar.activation(e2, e2, ACT.Exp).then_inc(gexp_done, 1)

                def group(g, it, lit):
                    for k in range(KD):
                        act.wait_ge(xg_psum, it * KD + (k + 1))
                        nc.scalar.activation(xg[:, k, :], ps[:, 6 + k % 2, 0:NE * CAP], ACT.Copy,
                                             scale=gain[:, gi, k:k + 1]).then_inc(xg_done, 1)
                    act.wait_ge(selt_psum, it + 1)
                    nc.scalar.activation(selT.rearrange("p q t n -> p (q t n)"), ps[:, 5, :], ACT.Copy
                                         ).then_inc(selt_done, 1)
                    for e in range(NE):
                        b = e % 2
                        act.wait_ge(gu_psum, it * NE + (e + 1))
                        nc.scalar.activation(sil[:, b, :], ps[:, b, 0:P], ACT.Silu).then_inc(silu_done, 1)
                        act.wait_ge(ht_psum, it * NE + (e + 1))
                        nc.scalar.activation(hT[:, b, :], ps[:, 4, 0:P], ACT.Copy).then_inc(ht_done, 1)
                        act.wait_ge(y_psum, it * NE + (e + 1))
                        r0 = CAP * (e % QUAD)
                        for c in (2, 3):
                            last = nc.scalar.activation(
                                yq[r0:r0 + CAP, e // QUAD, 256 * c:256 * (c + 1)],
                                ps[CAP * c:CAP * (c + 1), 2 + b, 0:256], ACT.Copy)
                        last.then_inc(y_act, 1)

                return passes(act, layer, before, group)

            n1 = moe(0, 0)
            its = act.snap(n1 * NG)

            norm_squares(2, its)
            store_transposed(2, [(2, xTkv), (3, xT)])
            act.wait_ge(zeroed, 2)

            def store_q(i):
                act.wait_ge(qt_psum, i + 1)
                t, m0 = i // 2, 4 * (i % 2)
                nc.scalar.activation(qbd[0:DH, m0:m0 + 4, :, 0, :],
                                     ps[0:DH, i, :].rearrange("p (m c q) -> p m c q", m=4, c=2),
                                     ACT.Copy, scale=SCALE).then_inc(qt_act, 1)

            def exp_scores(c):
                b = c % 2
                w = CHUNK if c == 0 else 2 * CHUNK
                act.wait_ge(max_done, c + 1)
                if c >= 2:
                    act.wait_ge(pt_psum, c - 1)
                else:
                    act.wait_ge(kv_done, 1)
                for m in range(PAIRS):
                    nc.scalar.activation(pB[:, b, m, 0:w],
                                         ps[:, 2 - 2 * b + m // 4, P * (m % 4):P * (m % 4) + w], ACT.Exp,
                                         bias=nmxB[:, b, m:m + 1], accum_out=sumB[:, b, m:m + 1])
                nc.scalar.activation(esB[:, b, :], esB[:, b, :], ACT.Exp).then_inc(p_exp, 1)

            def store_pT(c):
                act.wait_ge(pt_psum, c + 1)
                if c >= 2:
                    act.wait_ge(ob_psum, c - 1)
                for i in range(2):
                    last = nc.scalar.activation(
                        pT[:, c % 2, 4 * i:4 * i + 4, :].rearrange("p m n -> p (m n)"),
                        ps[:, 4 + i, :], ACT.Copy)
                last.then_inc(pt_done, 1)

            store_q(0)
            store_q(1)
            exp_scores(0)
            exp_scores(1)
            store_pT(0)
            store_pT(1)
            store_q(2)
            store_q(3)
            exp_scores(2)
            exp_scores(3)
            store_pT(2)
            store_pT(3)
            act.wait_ge(wo_psum, 8)
            act.dma_start(fgain, bc(final_norm.rearrange("(a n) -> a n", a=1), 0, P)
                          ).then_inc(fgain_in, 16)
            n2 = moe(1, its)
            norm_squares(4, act.snap((n1 + n2) * NG))

        @block.vector
        def _(dve):
            chain = [0]

            def link(ins):
                chain[0] += 1
                ins.then_inc(vchain, 1)
                dve.wait_ge(vchain, chain[0])

            def mark(ins):
                chain[0] += 1
                ins.then_inc(vchain, 1)
                return chain[0]

            V = nc.vector

            def store_transposed(n, gains):
                for t in range(T):
                    dve.wait_ge(xt_psum, T * n + t + 1)
                    for gi, dst in gains:
                        src = ps[:, 2 * t + 1, :].rearrange("p (k q) -> p k q", k=4)
                        d = dst[:, 4:8, P * t:P * (t + 1)]
                        if gi is None:
                            last = V.tensor_copy(d, src)
                        else:
                            last = V.tensor_tensor(d, src, bc(gain[:, gi, 4:8].unsqueeze(2), 2, P), ALU.mult)
                    last.then_inc(xt_dve, 1)

            V.memset(gpad[:, :, :], -3.0e38).then_inc(y_dve, 1)

            dve.wait_ge(rstd_done, 1)
            for t in range(T):
                V.tensor_scalar(xn[:, t, :], h[:, t, :], ss[:, 2, t:t + 1], None, ALU.mult
                                ).then_inc(xn_done, 1)
            dve.wait_ge(const_in, 32)
            store_transposed(0, [(0, xT)])
            for i in range(4):
                t, half = i % 2, i // 2
                dve.wait_ge(v_psum, i + 1)
                V.tensor_copy(v_rows[:, t, 512 * half:512 * (half + 1)], ps[:, 4 + i, :]).then_inc(v_done, 1)

            def both(c):
                return bc(c.unsqueeze(1), 1, 2)

            for i in range(PAIRS + 3):
                if 0 <= i - 2 < PAIRS:
                    m = i - 2
                    b = m % 2
                    zb = ps[:, 2 + 2 * b:4 + 2 * b, :]
                    dve.wait_ge(tail_psum, m + 1)
                    if m >= 2:
                        dve.wait_ge(o_psum, m - 1)
                    for a in range(2):
                        dg = zb[:, a, :].rearrange("p (k n) -> p k n", k=2)[:, :, 0:P]
                        wd = wA[:, b, a, :].rearrange("p (k n) -> p k n", k=3)[:, 0::2, :]
                        V.tensor_tensor(wd, dg, both(capc), ALU.min)
                    V.tensor_scalar(wA[:, b, :, P:2 * P], zb[:, :, P:2 * P], 0.0, None, ALU.min
                                    ).then_inc(arg_done, 1)
                if 0 <= i - 1 < PAIRS:
                    m = i - 1
                    b = m % 2
                    zb = ps[:, 2 + 2 * b:4 + 2 * b, :]
                    dve.wait_ge(zln_done, m + 1)
                    link(V.scalar_tensor_tensor(out=sp[:, b, :, :], in0=zb[:, :, 0:384], scalar=0.0,
                                                in1=za[:, b, :, :], op0=ALU.max, op1=ALU.add))
                    for a in range(2):
                        dg = sp[:, b, a, :].rearrange("p (k n) -> p k n", k=3)[:, 0::2, :]
                        last = V.tensor_tensor(dg, dg, both(maskc), ALU.mult)
                    last.then_inc(sp_done, 1)
                if 0 <= i - 3 < PAIRS:
                    m = i - 3
                    dve.wait_ge(o_psum, m + 1)
                    V.tensor_copy(oT[:, m, :], ps[:, 6 + m % 2, 0:SEQ]).then_inc(o_done, 1)

            def add_attention(layer, i):
                r = slice(512 * (i % 2), 512 * (i % 2 + 1))
                dve.wait_ge(wo_psum, 4 * layer + i + 1)
                V.tensor_tensor(h[:, i // 2, r], h[:, i // 2, r], ps[:, WO_BANKS[layer][i], :], ALU.add
                                ).then_inc(h_done, 1)

            for i in range(4):
                add_attention(0, i)

            def spread(x3, n):
                return bc(x3, 2, n)

            def route(layer):
                dve.wait_ge(lg_psum, layer + 1)
                lg = ps[:, 4, 0:T * 64].rearrange("p (t n) -> p t n", t=T)[:, :, 0:NG + EXP]
                dve.wait_ge(rstd_done, 2 + 2 * layer)
                for t in range(T):
                    for dst, c in ((gpad[:, t, 0:NG], slice(0, NG)), (logit[:, t, NG:], slice(NG, NG + EXP))):
                        last = V.scalar_tensor_tensor(out=dst, in0=lg[:, t, c], scalar=ss[:, 2, t:t + 1],
                                                      in1=rbias[:, layer, c], op0=ALU.mult, op1=ALU.add)
                link(last)
                for t in range(T):
                    last = V.max(gtop8[:, t, :], gpad[:, t, :])
                link(last)
                V.tensor_tensor(gexp[:, :, :], gpad[:, :, 0:NG], spread(gtop8[:, :, 0:1], NG), ALU.subtract
                                ).then_inc(gsub_done, 1)
                for t in range(T):
                    last = V.max_index(idx8[:, 0, t, :], gtop8[:, t, :], gpad[:, t, :])
                link(last)
                link(V.tensor_copy(gidx[:, :, :], idx8[:, 0, :, 0:1]))
                link(V.tensor_tensor(goh[:, :, :], bc(iota[:, 0:NG].unsqueeze(1), 1, T),
                                     spread(gidx[:, :, 0:1], NG), ALU.is_equal))
                link(V.tensor_tensor(prod[:, :, :, :],
                                     logit[:, :, NG:].rearrange("p t (g e) -> p t g e", g=NG),
                                     bc(goh[:, :, :].unsqueeze(3), 3, NE), ALU.mult))
                link(V.tensor_reduce(esel[:, :, :], prod.rearrange("p t g e -> p t e g"), AX.X, ALU.add))
                for t in range(T):
                    last = V.max(etop8[:, t, :], esel[:, t, :])
                link(last)
                V.tensor_tensor(e2.unsqueeze(2), etop8[:, :, 1:2], etop8[:, :, 0:1], ALU.subtract
                                ).then_inc(gsub_done, 1)
                for t in range(T):
                    last = V.max_index(idx8[:, 1, t, :], etop8[:, t, :], esel[:, t, :])
                found = mark(last)
                dve.wait_ge(gexp_done, 2 * layer + 1)
                summed = mark(V.tensor_reduce(gsum, gexp[:, :, :], AX.X, ALU.add))
                dve.wait_ge(vchain, found)
                link(V.tensor_copy(eidx[:, :, :], idx8[:, 1, :, 0:2]))
                for r in range(2):
                    last = V.tensor_tensor(oh[:, r, :, :], bc(iota[:, 0:NE].unsqueeze(1), 1, T),
                                           spread(eidx[:, :, r:r + 1], NE), ALU.is_equal)
                chosen = mark(last)
                dve.wait_ge(gexp_done, 2 * layer + 2)
                dve.wait_ge(vchain, summed)
                product = mark(V.scalar_tensor_tensor(out=w12[:, 0, :], in0=e2, scalar=1.0, in1=gsum,
                                                      op0=ALU.add, op1=ALU.mult))
                dve.wait_ge(vchain, chosen)
                both_experts = mark(V.tensor_tensor(msum[:, :, :], oh[:, 0, :, :], oh[:, 1, :, :], ALU.add))
                dve.wait_ge(vchain, product)
                first_share = mark(V.reciprocal(w12[:, 0, :], w12[:, 0, :]))

                def per_group(dst, x3):
                    return V.tensor_tensor(dst.rearrange("p t (g e) -> p t g e", g=NG),
                                           bc(goh[:, :, :].unsqueeze(3), 3, NE),
                                           bc(x3.unsqueeze(2), 2, NG), ALU.mult)

                dve.wait_ge(vchain, both_experts)
                per_group(member[:, :, :], msum[:, :, :]).then_inc(member_done, 1)
                dve.wait_ge(vchain, first_share)
                shares = mark(V.tensor_tensor(w12[:, 1, :], w12[:, 0, :], e2, ALU.mult))
                dve.wait_ge(member_done, layer + 1)
                base = mark(V.tensor_scalar(rank[:, :, :], member[:, :, :], -FAR, FAR, ALU.mult, ALU.add))
                dve.wait_ge(vchain, shares)
                for r in range(2):
                    last = V.tensor_tensor(oh[:, r, :, :], oh[:, r, :, :],
                                           spread(w12[:, r, :].unsqueeze(2), NE), ALU.mult)
                weighted = mark(last)
                dve.wait_ge(rank_psum, layer + 1)
                dve.wait_ge(vchain, base)
                mark(V.tensor_tensor(rank[:, :, :], rank[:, :, :],
                                     ps[:, 5, 0:T * EXP].rearrange("p (t n) -> p t n", t=T), ALU.add))
                dve.wait_ge(vchain, weighted)
                weights = mark(V.tensor_tensor(wsum[:, :, :], oh[:, 0, :, :], oh[:, 1, :, :], ALU.add))
                fullest = mark(V.reduce_max(cnt[:, 0:1], ps[:, 5, T * EXP:(T + 1) * EXP], AX.X))
                dve.wait_ge(vchain, weights)
                placed = mark(per_group(tokw[:, :, :], wsum[:, :, :]))
                dve.wait_ge(vchain, fullest)
                V.tensor_scalar(thr[:, 0:N_THR], cst[:, C_THR:C_THR + N_THR], cnt[:, 0:1], 1.0,
                                ALU.is_lt, ALU.add, accum_out=cnt[:, 1:2]).then_inc(counted, 1)
                dve.wait_ge(vchain, placed)

            def moe(layer, before):
                store_transposed(1 + 2 * layer, [(None, xT)])
                route(layer)

                def add_quad(it, q):
                    for i in range(4):
                        t, half = i // 2, i % 2
                        r = slice(512 * half, 512 * (half + 1))
                        dve.wait_ge(comb_psum, it * 8 + (4 * q + i + 1))
                        V.tensor_tensor(h[:, t, r], h[:, t, r], ps[:, 6 + i % 2, :], ALU.add
                                        ).then_inc(added[t], 1)

                def group(g, it, lit):
                    cols = bass.ds(g * NE, NE)
                    slots = bc(iota.unsqueeze(1), 1, NE)
                    for t in range(T):
                        last = V.tensor_tensor(selg[:, t, :].rearrange("p (e s) -> p e s", e=NE),
                                               slots, bc(rank[:, t, cols].unsqueeze(2), 2, CAP),
                                               ALU.is_equal)
                    last.then_inc(selg_done, 1)
                    dve.wait_ge(selg_done, it + 1)
                    for t in range(T):
                        last = V.tensor_tensor(selw[:, t, :].rearrange("p (e s) -> p e s", e=NE),
                                               selg[:, t, :].rearrange("p (e s) -> p e s", e=NE),
                                               bc(tokw[:, t, cols].unsqueeze(2), 2, CAP),
                                               ALU.mult)
                    last.then_inc(selw_done, 1)
                    V.tensor_scalar(rank[:, :, cols], rank[:, :, cols], float(-CAP), None, ALU.add)
                    for e in range(NE):
                        b = e % 2
                        dve.wait_ge(silu_done, it * NE + (e + 1))
                        V.tensor_tensor(hact[:, b, :], sil[:, b, :], ps[:, b, P:2 * P], ALU.mult
                                        ).then_inc(hact_done, 1)
                        if e == QUAD:
                            add_quad(it, 0)
                        dve.wait_ge(y_psum, it * NE + (e + 1))
                        r0 = CAP * (e % QUAD)
                        for c in (0, 1):
                            last = V.tensor_copy(yq[r0:r0 + CAP, e // QUAD, 256 * c:256 * (c + 1)],
                                                 ps[CAP * c:CAP * (c + 1), 2 + b, 0:256])
                        last.then_inc(y_dve, 1)
                    add_quad(it, 1)

                return passes(dve, layer, before, group)

            n1 = moe(0, 0)
            its = dve.snap(n1 * NG)

            store_transposed(2, [(2, xTkv), (3, xT)])

            def rope(dst, src, tmp, t, nh):
                hd = DH // 2
                for o, i, c0, c in ((dst, src, C_COS, slice(0, DH)),
                                    (tmp[:, :, 0:hd], src[:, :, hd:DH], C_SIN, slice(0, hd)),
                                    (tmp[:, :, hd:DH], src[:, :, 0:hd], C_SIN, slice(hd, DH))):
                    angles = cst[:, c0 + DH * t + c.start:c0 + DH * t + c.stop]
                    last = V.scalar_tensor_tensor(out=o, in0=i, scalar=ss[:, 2, t:t + 1],
                                                  in1=bc(angles.unsqueeze(1), 1, nh),
                                                  op0=ALU.mult, op1=ALU.mult)
                return last

            def rope_q(i):
                dve.wait_ge(q_psum, i + 1)
                if i >= 2:
                    dve.wait_ge(rope_done, i - 1)
                t, half = i // 2, i % 2
                rope(*(a.rearrange("p (h d) -> p h d", h=8)
                       for a in (q_rows[:, t, 512 * half:512 * (half + 1)], ps[:, 6 + half, :],
                                 ropes[:, half, :])), t, 8).then_inc(rope_dve, 1)

            def store_q(i):
                dve.wait_ge(qt_psum, i + 1)
                t, m0 = i // 2, 4 * (i % 2)
                V.tensor_scalar(qbd[DH:P, m0:m0 + 4, :, 1, :],
                                ps[DH:P, i, :].rearrange("p (m c q) -> p m c q", m=4, c=2),
                                SCALE, None, ALU.mult).then_inc(qt_dve, 1)

            def scored(c):
                b = 2 - 2 * (c % 2)
                w = CHUNK if c == 0 else 2 * CHUNK
                return ps[:, b:b + 2, :].rearrange("p x (m k) -> p (x m) k", m=4)[:, :, 0:w], w

            def find_max(c):
                b = c % 2
                sc, w = scored(c)
                dve.wait_ge(s_psum, c + 1)
                link(V.tensor_reduce(mxB[:, b, :], sc, AX.X, ALU.max))
                link(V.tensor_tensor(mxB[:, b, :], mxB[:, b, :], sinks[:, :], ALU.max))
                V.tensor_scalar(nmxB[:, b, :], mxB[:, b, :], -1.0, None, ALU.mult)
                V.tensor_tensor(esB[:, b, :], sinks[:, :], mxB[:, b, :], ALU.subtract
                                ).then_inc(max_done, 1)

            def normalise(c):
                b = c % 2
                _, w = scored(c)
                dve.wait_ge(p_exp, c + 1)
                link(V.tensor_tensor(sumB[:, b, :], sumB[:, b, :], esB[:, b, :], ALU.add))
                link(V.reciprocal(sumB[:, b, :], sumB[:, b, :]))
                V.tensor_tensor(pB[:, b, :, 0:w], pB[:, b, :, 0:w],
                                bc(sumB[:, b, :].unsqueeze(2), 2, w), ALU.mult).then_inc(p_done, 1)

            def store_o(c):
                dve.wait_ge(ob_psum, c + 1)
                V.tensor_copy(oT[:, :, CHUNK * c:CHUNK * (c + 1)],
                              ps[:, 6, :].rearrange("p (m q) -> p m q", m=PAIRS)).then_inc(ob_done, 1)

            kvt = ps[:, 4, :].rearrange("p (t n) -> p t n", t=T)
            for a in range(2):
                V.tensor_copy(sinks[DH * a:DH * (a + 1), :],
                              sink16[DH * a:DH * (a + 1), :].rearrange("p (m a) -> p m a", a=2)[:, :, a])
            dve.wait_ge(rstd_done, 3)
            dve.wait_ge(kv_psum, 1)
            for t in range(T):
                ka, kb = (kr[:, r, P * t:P * (t + 1)].rearrange("p (h d) -> p h d", h=KVH)
                          for r in range(2))
                link(rope(ka, kvt[:, t, 0:P].rearrange("p (h d) -> p h d", h=KVH), kb, t, KVH))
                for a in range(2):
                    last = V.tensor_tensor(k2[:, t, :, a, :], ka, kb, ALU.add)
            for r, win, r_in, t in ((slice(0, P), 0, slice(0, P), 0), (slice(0, P), 2, slice(0, P), 1),
                                    (slice(0, DH), 1, slice(DH, P), 0), (slice(DH, P), 1, slice(0, DH), 1)):
                last = V.tensor_scalar(vwin[r, win, :], kvt[r_in, t, P:2 * P], ss[r_in, 2, t:t + 1], None,
                                       ALU.mult)
            last.then_inc(kv_done, 1)
            rope_q(0)
            rope_q(1)
            dve.wait_ge(kt_psum, 1)
            V.tensor_copy(kdup.rearrange("p h k -> p (h k)"), ps[:, 5, :]).then_inc(kt_done, 1)
            dve.wait_ge(zeroed, 2)
            store_q(0)
            store_q(1)
            rope_q(2)
            find_max(0)
            find_max(1)
            normalise(0)
            normalise(1)
            rope_q(3)
            dve.wait_ge(rope_done, 4)
            store_o(0)
            store_q(2)
            store_q(3)
            store_o(1)
            find_max(2)
            find_max(3)
            normalise(2)
            normalise(3)
            add_attention(1, 0)
            store_o(2)
            store_o(3)
            for i in range(1, 4):
                add_attention(1, i)
            moe(1, its)
            dve.wait_ge(rstd_done, 5)
            dve.wait_ge(fgain_in, 16)
            for t in range(T):
                V.scalar_tensor_tensor(out=xn[:, t, :], in0=h[:, t, :], scalar=ss[:, 2, t:t + 1],
                                       in1=fgain, op0=ALU.mult, op1=ALU.mult).then_inc(out_done, 1)

        @block.tensor
        def _(pe):
            MM = nc.tensor.matmul

            def transpose_rows(n, its=None):
                src = xn if n == 0 else h
                for t in range(T):
                    if n == 0:
                        pe.wait_ge(xn_done, t + 1)
                    else:
                        rows_stand(pe, n, t, its)
                    for k in range(KD):
                        last = nc.tensor.transpose(ps[:, 2 * t + k // 4, P * (k % 4):P * (k % 4 + 1)],
                                                   src[:, t, k::KD], ident)
                    last.then_inc(xt_psum, 1)

            def xt_stands(n, t):
                pe.wait_ge(xt_act, T * n + t + 1)
                pe.wait_ge(xt_dve, T * n + t + 1)

            pe.wait_ge(const_in, 32)
            transpose_rows(0)
            for i in range(4):
                t, half = i % 2, i // 2
                xt_stands(0, t)
                wait_a(pe, half)
                wv = slot(slot_a(half)).rearrange("p (k n) -> p k n", k=KD)
                for k in range(KD):
                    last = MM(ps[:, 4 + i, :], xT[:, k, P * t:P * (t + 1)], wv[:, k, :],
                              start=k == 0, stop=k == KD - 1)
                last.then_inc(v_psum, 1)

            def project_out(layer, i, its=None, m0=0, m1=KD):
                t, half = i // 2, i % 2
                if m0 == 0 and layer == 0:
                    wait_a(pe, 6 + half)
                elif m0 == 0:
                    wait_b(pe, 3 + half, its)
                w = slot(slot_b(3 + half) if layer else slot_a(6 + half)).rearrange("p (m n) -> p m n", m=KD)
                for m in range(m0, m1):
                    last = MM(ps[:, WO_BANKS[layer][i], :], oT[:, m, P * t:P * (t + 1)], w[:, m, :],
                              start=m == 0, stop=m == KD - 1)
                if m1 == KD:
                    last.then_inc(wo_psum, 1)

            for i in range(PAIRS + 3):
                if i < PAIRS:
                    m = i
                    wait_a(pe, 2 + m // 2)
                    if m >= 2:
                        pe.wait_ge(qk_done, m - 1)
                    w = slot(slot_a(2 + m // 2)).rearrange("p (k n) -> p k n", k=KD)
                    for j in range(2):
                        for k in range(KD):
                            c0 = 256 * j + P * (m % 2)
                            last = MM(ps[:, m % 2, SEQ * j:SEQ * (j + 1)], w[:, k, c0:c0 + P], xT[:, k, :],
                                      start=k == 0, stop=k == KD - 1)
                    last.then_inc(qk_psum, 1)
                if i == PAIRS:
                    pe.wait_ge(o_done, 4)
                    pe.wait_ge(qk_done, PAIRS - 1)
                    project_out(0, 0, None, 0, 4)
                    pe.wait_ge(qk_done, PAIRS)
                    project_out(0, 1, None, 0, 2)
                if 0 <= i - 1 < PAIRS:
                    m = i - 1
                    b = m % 2
                    pe.wait_ge(qk_done, m + 1)
                    if m < 2:
                        pe.wait_ge(v_done, 2 * b + 2 if b == 0 else 4)
                    else:
                        pe.wait_ge(arg_done, m - 1)
                    for a in range(2):
                        z = ps[:, 2 + 2 * b + a, :]
                        MM(z[:, 0:SEQ], kz[:, b, a, 0:P], qT[:, b, :], start=True, stop=False,
                           skip_group_check=True)
                        last = MM(z[:, SEQ:SEQ + P], kz[:, b, a, P:SEQ], qT[:, b, P:SEQ], start=False,
                                  stop=False, skip_group_check=True)
                    last.then_inc(z_psum, 1)
                if i == PAIRS + 1:
                    pe.wait_ge(o_done, 5)
                    project_out(0, 1, None, 2, 5)
                if 0 <= i - 2 < PAIRS:
                    m = i - 2
                    b = m % 2
                    pe.wait_ge(sp_done, m + 1)
                    for a in range(2):
                        z = ps[:, 2 + 2 * b + a, :]
                        s0 = sp[:, b, a, :]
                        MM(z[:, SEQ:SEQ + P], ntri, s0[:, SEQ:SEQ + P], start=False, stop=False,
                           skip_group_check=True)
                        MM(z[:, 0:SEQ], ntri, s0[:, 0:SEQ], start=False, stop=False, skip_group_check=True)
                        last = MM(z[:, P:SEQ], nones, s0[:, SEQ:SEQ + P], start=False, stop=True,
                                  skip_group_check=True)
                    last.then_inc(tail_psum, 1)
                if 0 <= i - 3 < PAIRS:
                    m = i - 3
                    b = m % 2
                    pe.wait_ge(w_done, m + 1)
                    pe.wait_ge(v_done, 4)
                    if m >= 2:
                        pe.wait_ge(o_done, m - 1)
                    for kt in range(2):
                        for a in range(2):
                            hd = 2 * m + a
                            last = MM(ps[DH * a:DH * (a + 1), 6 + b, P * kt:SEQ],
                                      v_rows[:, kt, DH * hd:DH * (hd + 1)],
                                      wA[:, b, a, SEQ * kt:SEQ if kt == 0 else SEQ + P],
                                      start=kt == 0, stop=kt == 1, skip_group_check=True)
                    last.then_inc(o_psum, 1)

                if i == PAIRS + 1:
                    pe.wait_ge(o_done, 6)
                    project_out(0, 1, None, 5, 6)
                    project_out(0, 0, None, 4, 6)

            pe.wait_ge(o_done, PAIRS)
            for i in range(4):
                project_out(0, i, None, 6 if i < 2 else 0)

            def moe(layer, before):
                transpose_rows(1 + 2 * layer)
                pe.wait_ge(prepared, 1)
                for t in range(T):
                    xt_stands(1 + 2 * layer, t)
                    for k in range(KD):
                        last = MM(ps[:, 4, 64 * t:64 * t + NG + EXP], xT[:, k, P * t:P * (t + 1)],
                                  wr[:, layer, k, :], start=k == 0, stop=k == KD - 1)
                last.then_inc(lg_psum, 1)
                pe.wait_ge(member_done, layer + 1)
                for t in range(T + 1):
                    for u in range(min(t + 1, T)):
                        last = MM(ps[:, 5, EXP * t:EXP * (t + 1)], counting[:, 0 if u == t else 1, :],
                                  member[:, u, :], start=u == 0, stop=u == min(t, T - 1))
                last.then_inc(rank_psum, 1)

                def combine(it, q):
                    pe.wait_ge(y_act, it * NE + (QUAD * (q + 1) + 1))
                    pe.wait_ge(y_dve, it * NE + (QUAD * (q + 1) + 1))
                    if q == 0:
                        pe.wait_ge(selt_done, it + 1)
                    for i in range(4):
                        t, half = i // 2, i % 2
                        if i >= 2:
                            pe.wait_ge(added[0], it * 4 + (2 * q + half + 1))
                        elif q == 1:
                            pe.wait_ge(added[1], it * 4 + (half + 1))
                        MM(ps[:, 6 + i % 2, :], selT[:, q, t, :], yq[:, q, 512 * half:512 * (half + 1)],
                           start=True, stop=True).then_inc(comb_psum, 1)

                def group(g, it, lit):
                    pe.wait_ge(selg_done, it + 1)
                    pe.wait_ge(xn_done, T * (layer + 2))
                    def gather(ks):
                        for k in ks:
                            if k >= 2:
                                pe.wait_ge(xg_done, it * KD + (k - 1))
                            for t in range(T):
                                last = MM(ps[:, 6 + k % 2, 0:NE * CAP], xn[:, t, k::KD],
                                          selg[:, t, :], start=t == 0, stop=t == T - 1)
                            last.then_inc(xg_psum, 1)

                    def gate_up(e, half):
                        s = 3 * e + half
                        wait_m(pe, layer, s, before, lit)
                        w = slot(slot_m(layer, s)).rearrange("p (u k f) -> p u k f", u=2, k=4)
                        for k in range(4):
                            for j in range(4):
                                kk = 4 * half + k
                                last = MM(ps[CAP * j:CAP * (j + 1), e % 2, 0:2 * P].rearrange(
                                              "p (u f) -> p u f", u=2),
                                          xg[:, kk, CAP * e:CAP * (e + 1)],
                                          w[:, :, k, P * j:P * (j + 1)],
                                          start=kk == 0, stop=kk == KD - 1, skip_group_check=True)
                        last.then_inc(gu_psum if half else gu_half, 1)

                    gather(range(KD // 2))
                    pe.wait_ge(xg_done, it * KD + KD // 2)
                    gate_up(0, 0)
                    gather(range(KD // 2, KD))
                    pe.wait_ge(selw_done, it + 1)
                    for q in range(2):
                        for t in range(T):
                            last = nc.tensor.transpose(ps[:, 5, P * (2 * q + t):P * (2 * q + t + 1)],
                                                       selw[:, t, P * q:P * (q + 1)], ident)
                    last.then_inc(selt_psum, 1)
                    pe.wait_ge(xg_done, it * KD + KD)
                    for e in range(NE):
                        b = e % 2
                        if e:
                            gate_up(e, 0)
                        gate_up(e, 1)
                        if e == QUAD:
                            combine(it, 0)
                        pe.wait_ge(hact_done, it * NE + (e + 1))
                        nc.tensor.transpose(ps[:, 4, 0:P], hact[:, b, :], ident).then_inc(ht_psum, 1)
                        pe.wait_ge(ht_done, it * NE + (e + 1))
                        pe.wait_ge(y_act, it * NE + (e + 1))
                        pe.wait_ge(y_dve, it * NE + (e + 1))
                        wait_m(pe, layer, 3 * e + 2, before, lit)
                        w = slot(slot_m(layer, 3 * e + 2)).rearrange("p (j n) -> p j n", j=4)
                        for j in range(4):
                            for c in range(4):
                                last = MM(ps[CAP * c:CAP * (c + 1), 2 + b, 0:256],
                                          hT[:, b, CAP * j:CAP * (j + 1)],
                                          w[:, j, 256 * c:256 * (c + 1)],
                                          start=j == 0, stop=j == 3, skip_group_check=True)
                        last.then_inc(y_psum, 1)
                    combine(it, 1)

                return passes(pe, layer, before, group)

            n1 = moe(0, 0)
            its = pe.snap(n1 * NG)

            transpose_rows(2, its)

            def project_q(i, k0=0, k1=KD):
                t, half = i // 2, i % 2
                if k0 == 0:
                    wait_b(pe, 1 + half, its)
                if k0 == 0 and i >= 2:
                    pe.wait_ge(rope_dve, i - 1)
                w = slot(slot_b(1 + half)).rearrange("p (k n) -> p k n", k=KD)
                for k in range(k0, k1):
                    last = MM(ps[:, 6 + i % 2, :], xT[:, k, P * t:P * (t + 1)], w[:, k, :],
                              start=k == 0, stop=k == KD - 1)
                if k1 == KD:
                    last.then_inc(q_psum, 1)

            def transpose_q(t):
                pe.wait_ge(rope_done, 2 * (t + 1))
                if t == 1:
                    pe.wait_ge(p_exp, 1)
                for half in range(2):
                    for m in range(4):
                        mm = 4 * half + m
                        last = nc.tensor.transpose(ps[:, 2 * t + half, P * m:P * (m + 1)],
                                                   q_rows[:, t, P * mm:P * (mm + 1)], ident)
                    last.then_inc(qt_psum, 1)

            def scores(c):
                b = 2 - 2 * (c % 2)
                if c < 3:
                    pe.wait_ge(qt_act, 2 * (c // 2 + 1))
                    pe.wait_ge(qt_dve, 2 * (c // 2 + 1))
                else:
                    pe.wait_ge(p_exp, 2)
                k0 = max(0, CHUNK * (c - 1))
                for m in range(PAIRS):
                    last = MM(ps[:, b + m // 4, P * (m % 4):P * (m % 4 + 1)],
                              qbd[:, m, c % 2, :, :].rearrange("p a q -> p (a q)"),
                              kdup[:, m // (PAIRS // KVH), k0:k0 + P], start=True, stop=True)
                last.then_inc(s_psum, 1)

            def transpose_p(c):
                pe.wait_ge(p_done, c + 1)
                if c == 0:
                    pe.wait_ge(zeroed, 3)
                else:
                    pe.wait_ge(pt_done, c)
                for m in range(PAIRS):
                    last = nc.tensor.transpose(ps[:, 4 + m // 4, P * (m % 4):P * (m % 4 + 1)],
                                               pB[:, c % 2, m, :], ident)
                last.then_inc(pt_psum, 1)

            def weigh_v(c):
                pe.wait_ge(pt_done, c + 1)
                if c >= 1:
                    pe.wait_ge(ob_done, c)
                else:
                    pe.wait_ge(rope_dve, 3)
                win = max(0, c - 1)
                for hk in range(KVH):
                    for a in range(2):
                        last = MM(ps[DH * a:DH * (a + 1), 6, 256 * hk:256 * (hk + 1)].rearrange(
                                      "p (m q) -> p m q", m=4),
                                  vwin[:, win, DH * hk:DH * (hk + 1)],
                                  pT[:, c % 2, 4 * hk:4 * hk + 4, DH * a:DH * (a + 1)],
                                  start=True, stop=True, skip_group_check=True)
                last.then_inc(ob_psum, 1)

            wait_b(pe, 0, its)
            w = slot(slot_b(0))[:, 0:KD * 256].rearrange("p (k n) -> p k n", k=KD)
            for t in range(T):
                xt_stands(2, t)
                for k in range(KD):
                    last = MM(ps[:, 4, 256 * t:256 * (t + 1)], xTkv[:, k, P * t:P * (t + 1)], w[:, k, :],
                              start=k == 0, stop=k == KD - 1)
            last.then_inc(kv_psum, 1)
            project_q(0)
            project_q(1)
            pe.wait_ge(kv_done, 1)
            for hk in range(KVH):
                for t in range(T):
                    c0 = SEQ * hk + P * t
                    last = nc.tensor.transpose(ps[:, 5, c0:c0 + P],
                                               k2[:, t, hk, :, :].rearrange("p a d -> p (a d)"), ident)
            last.then_inc(kt_psum, 1)
            project_q(2, 0, KD // 2)
            transpose_q(0)
            project_q(2, KD // 2, KD)
            pe.wait_ge(kt_done, 1)
            scores(0)
            scores(1)
            project_q(3)
            transpose_p(0)
            transpose_p(1)
            weigh_v(0)
            transpose_q(1)
            weigh_v(1)
            scores(2)
            pe.wait_ge(ob_done, 2)
            pe.wait_ge(rope_dve, 4)
            project_out(1, 0, its, 0, 3)
            scores(3)
            project_out(1, 0, its, 3)
            pe.wait_ge(p_exp, 3)
            project_out(1, 1, its, 0, 2)
            transpose_p(2)
            project_out(1, 1, its, 2, 4)
            weigh_v(2)
            transpose_p(3)
            project_out(1, 1, its, 4, 6)
            weigh_v(3)
            project_out(1, 1, its, 6)
            pe.wait_ge(ob_done, 4)
            project_out(1, 2, its)
            pe.wait_ge(h_done, 4 + 1)
            project_out(1, 3, its)
            moe(1, its)


N_PARAMS = 4 + 8 + 1

_INS = ["x", "a_norm", "a_w_qkv", "a_w_o", "kv_norm", "kv_w", "b_norm", "b_w_q", "b_sinks", "b_w_o",
        "ffn_norm", "moe_w_group", "moe_b_group", "moe_w_router", "moe_b_router", "moe_w_gate",
        "moe_w_up", "moe_w_down", "final_norm"]


def kernel(**inputs):
    import concourse.bacc as bacc
    from concourse.bass_utils import run_bass_kernel_spmd

    nc = bacc.Bacc("TRN2", target_bir_lowering=False, num_devices=1)
    arrays = {f"in_{n}": np.ascontiguousarray(inputs[n]) for n in _INS}
    arrays["in_consts"] = shape_constants()
    args = [nc.dram_tensor(n, a.shape, mybir.dt.from_np(a.dtype), kind="ExternalInput").ap()
            for n, a in arrays.items()]
    args.append(nc.dram_tensor("out_0", (1, SEQ, D), F32, kind="ExternalOutput").ap())
    build(nc, *args)
    r = run_bass_kernel_spmd(nc, [arrays], core_ids=[0])
    return r.results[0]["out_0"]
```
